# Optimizing a Trainium2 kernel written in Bass

```python
import math
import jax, jax.numpy as jnp
from jax import lax
import numpy as np

D_MODEL = 1024
BATCH = 1
SEQ = 256
DEPTH = 1
DEC_BATCH = 8
DEC_SEQ = 8
PAST_LEN = 2048
PAGE_SIZE = 128

D_CONF = D_MODEL
CONF_KERNEL = 31
D_SSM = D_MODEL
SSM_HEAD_DIM = 64
SSM_HEADS = D_SSM // SSM_HEAD_DIM
SSM_GROUPS = 2
SSM_HPG = SSM_HEADS // SSM_GROUPS
SSM_STATE = 128
SSM_CONV = 4
SSD_CHUNK = 128
XBC_DIM = D_SSM + 2 * SSM_GROUPS * SSM_STATE
D_MIX = D_CONF + D_SSM
IN_COLS = 2 * D_CONF + D_SSM + XBC_DIM + SSM_HEADS
MOE_GROUPS = 4
EXPERTS_PER_GROUP = 8
N_EXPERTS = MOE_GROUPS * EXPERTS_PER_GROUP
TOP_K_INNER = 2
D_EXPERT = D_MODEL // 2
EPS = 1e-6

kernel_name = 'hymba_conformer_ssd_hmoe_step'

def rmsnorm(x, g):
    xf = x.astype(jnp.float32)
    y = xf * lax.rsqrt(jnp.mean(xf * xf, axis=-1, keepdims=True) + EPS)
    return (y * g.astype(jnp.float32)).astype(x.dtype)

def layernorm(x, g, b):
    xf = x.astype(jnp.float32)
    mu = jnp.mean(xf, axis=-1, keepdims=True)
    xc = xf - mu
    y = xc * lax.rsqrt(jnp.mean(xc * xc, axis=-1, keepdims=True) + EPS)
    return (y * g.astype(jnp.float32) + b.astype(jnp.float32)).astype(x.dtype)

def causal_dwconv(buf, u, w, b):
    full = jnp.concatenate([buf.astype(u.dtype), u], axis=1)
    out = lax.conv_general_dilated(full, w[:, None, :].astype(u.dtype), window_strides=(1,),
                                   padding='VALID', dimension_numbers=('NWC', 'WIO', 'NWC'),
                                   feature_group_count=u.shape[-1])
    new_buf = full[:, full.shape[1] - (w.shape[0] - 1):]
    return out + b.astype(u.dtype), new_buf

def ssd_scan(x, dt, a, b_in, c_in, h0, chunk):
    bt, L = x.shape[0], x.shape[1]
    nc = L // chunk
    f32 = jnp.float32
    def chunked(t):
        return t.astype(f32).reshape((bt, nc, chunk) + t.shape[2:])
    xc, dtc, bc, cc = chunked(x), chunked(dt), chunked(b_in), chunked(c_in)
    acum = jnp.cumsum(dtc * a.astype(f32), axis=2)
    xdt = xc * dtc[..., None]
    causal = jnp.tril(jnp.ones((chunk, chunk), dtype=bool))[None, None, :, :, None, None]
    seg = acum[:, :, :, None] - acum[:, :, None, :]
    decay = jnp.exp(jnp.where(causal, seg, -jnp.inf))
    cb = jnp.einsum('bcign,bcjgn->bcijg', cc, bc)
    y_diag = jnp.einsum('bcijg,bcijgr,bcjgrp->bcigrp', cb, decay, xdt)
    decay_to_end = jnp.exp(acum[:, :, -1:] - acum)
    states = jnp.einsum('bcjgn,bcjgr,bcjgrp->bcgrpn', bc, decay_to_end, xdt)
    chunk_decay = jnp.exp(acum[:, :, -1])
    def step(h, inp):
        s, d = inp
        return d[..., None, None] * h + s, h
    h_last, h_prev = lax.scan(step, h0.astype(f32),
                              (jnp.moveaxis(states, 1, 0), jnp.moveaxis(chunk_decay, 1, 0)))
    h_prev = jnp.moveaxis(h_prev, 0, 1)
    y_off = jnp.einsum('bcign,bcigr,bcgrpn->bcigrp', cc, jnp.exp(acum), h_prev)
    y = (y_diag + y_off).reshape(x.shape)
    return y.astype(x.dtype), h_last.astype(h0.dtype)

def mixer(h, conf_buf, ssm_buf, ssm_h, w_in, conf_dw_w, conf_dw_b, conf_ln_g, conf_ln_b,
          ssm_conv_w, ssm_conv_b, dt_bias, a_log, d_skip, ssm_norm_g, w_out):
    bt, L, _ = h.shape
    proj = jnp.einsum('bld,de->ble', h, w_in.astype(h.dtype))
    i1, i2, i3, i4 = D_CONF, 2 * D_CONF, 2 * D_CONF + D_SSM, 2 * D_CONF + D_SSM + XBC_DIM
    u_a, u_b, z, xbc, dt_raw = proj[..., :i1], proj[..., i1:i2], proj[..., i2:i3], proj[..., i3:i4], proj[..., i4:]
    u = u_a * jax.nn.sigmoid(u_b)
    v, conf_buf_new = causal_dwconv(conf_buf, u, conf_dw_w, conf_dw_b)
    v = jax.nn.silu(layernorm(v, conf_ln_g, conf_ln_b))
    xbc_c, ssm_buf_new = causal_dwconv(ssm_buf, xbc, ssm_conv_w, ssm_conv_b)
    xbc_c = jax.nn.silu(xbc_c)
    xs = xbc_c[..., :D_SSM].reshape(bt, L, SSM_GROUPS, SSM_HPG, SSM_HEAD_DIM)
    bs = xbc_c[..., D_SSM:D_SSM + SSM_GROUPS * SSM_STATE].reshape(bt, L, SSM_GROUPS, SSM_STATE)
    cs = xbc_c[..., D_SSM + SSM_GROUPS * SSM_STATE:].reshape(bt, L, SSM_GROUPS, SSM_STATE)
    dt = jax.nn.softplus(dt_raw.astype(jnp.float32) + dt_bias.astype(jnp.float32))
    dt = dt.reshape(bt, L, SSM_GROUPS, SSM_HPG)
    a = -jnp.exp(a_log.astype(jnp.float32)).reshape(SSM_GROUPS, SSM_HPG)
    h0 = ssm_h.reshape(bt, SSM_GROUPS, SSM_HPG, SSM_HEAD_DIM, SSM_STATE)
    chunk = math.gcd(L, SSD_CHUNK)
    y, h_new = ssd_scan(xs, dt, a, bs, cs, h0, chunk)
    y = y + d_skip.astype(y.dtype).reshape(SSM_GROUPS, SSM_HPG, 1) * xs
    yz = (y.reshape(bt, L, D_SSM) * jax.nn.silu(z)).reshape(bt, L, SSM_GROUPS, D_SSM // SSM_GROUPS)
    yz = rmsnorm(yz, jnp.ones((D_SSM // SSM_GROUPS,), jnp.float32)).reshape(bt, L, D_SSM)
    y_ssm = yz * ssm_norm_g.astype(yz.dtype)
    out = jnp.einsum('ble,ed->bld', jnp.concatenate([v, y_ssm], axis=-1), w_out.astype(h.dtype))
    h_new = h_new.reshape(bt, SSM_HEADS, SSM_HEAD_DIM, SSM_STATE)
    return out, conf_buf_new, ssm_buf_new, h_new

def hier_moe(h, rg_w, rg_b, re_w, re_b, w_gate, w_up, w_down):
    shp = h.shape
    t = h.reshape(-1, shp[-1])
    tf = t.astype(jnp.float32)
    lg = tf @ rg_w.astype(jnp.float32) + rg_b.astype(jnp.float32)
    pg = jax.nn.softmax(lg, axis=-1)
    grp = jnp.argmax(lg, axis=-1)
    g1 = jnp.take_along_axis(pg, grp[:, None], axis=-1)
    le_all = jnp.einsum('td,gde->tge', tf, re_w.astype(jnp.float32)) + re_b.astype(jnp.float32)
    le = jnp.take_along_axis(le_all, grp[:, None, None], axis=1)[:, 0]
    top_v, top_i = lax.top_k(le, TOP_K_INNER)
    g2 = jax.nn.softmax(top_v, axis=-1)
    eid = grp[:, None] * EXPERTS_PER_GROUP + top_i
    combine = jnp.sum(jax.nn.one_hot(eid, N_EXPERTS, dtype=jnp.float32) * (g1 * g2)[..., None], axis=1)
    combine = combine.astype(t.dtype)
    acc = jnp.zeros_like(t)
    for e in range(N_EXPERTS):
        hid = jax.nn.silu(t @ w_gate[e].astype(t.dtype)) * (t @ w_up[e].astype(t.dtype))
        acc = acc + combine[:, e:e + 1] * (hid @ w_down[e].astype(t.dtype))
    return acc.reshape(shp)

def setup_inputs(seed: int = 0) -> dict:
    key = jax.random.key(seed)
    ks = jax.random.split(key, 32)
    n = jax.random.normal
    f = jnp.float32
    dt0 = jnp.exp(jax.random.uniform(ks[10], (DEPTH, SSM_HEADS), f, math.log(1e-3), math.log(1e-1)))
    return {
        'x_prompt': n(ks[0], (BATCH, SEQ, D_MODEL), f),
        'x_sample': n(ks[1], (DEC_BATCH, DEC_SEQ, D_MODEL), f),
        'state_conf_conv': n(ks[2], (DEPTH, DEC_BATCH, CONF_KERNEL - 1, D_CONF), f),
        'state_ssm_conv': n(ks[3], (DEPTH, DEC_BATCH, SSM_CONV - 1, XBC_DIM), f),
        'state_ssm': 0.5 * n(ks[4], (DEPTH, DEC_BATCH, SSM_HEADS, SSM_HEAD_DIM, SSM_STATE), f),
        'ln_mix': 1.0 + 0.02 * n(ks[5], (DEPTH, D_MODEL), f),
        'w_in': n(ks[6], (DEPTH, D_MODEL, IN_COLS), f) * D_MODEL ** -0.5,
        'conf_dw_w': n(ks[7], (DEPTH, CONF_KERNEL, D_CONF), f) * CONF_KERNEL ** -0.5,
        'conf_dw_b': 0.02 * n(ks[8], (DEPTH, D_CONF), f),
        'conf_ln_g': 1.0 + 0.02 * n(ks[9], (DEPTH, D_CONF), f),
        'conf_ln_b': 0.02 * n(ks[11], (DEPTH, D_CONF), f),
        'ssm_conv_w': n(ks[12], (DEPTH, SSM_CONV, XBC_DIM), f) * SSM_CONV ** -0.5,
        'ssm_conv_b': 0.02 * n(ks[13], (DEPTH, XBC_DIM), f),
        'ssm_dt_bias': dt0 + jnp.log(-jnp.expm1(-dt0)),
        'ssm_a_log': jnp.log(jax.random.uniform(ks[14], (DEPTH, SSM_HEADS), f, 1.0, 16.0)),
        'ssm_d': 1.0 + 0.1 * n(ks[15], (DEPTH, SSM_HEADS), f),
        'ssm_norm_g': 1.0 + 0.02 * n(ks[16], (DEPTH, D_SSM), f),
        'w_out': n(ks[17], (DEPTH, D_MIX, D_MODEL), f) * D_MIX ** -0.5,
        'ln_ffn': 1.0 + 0.02 * n(ks[18], (DEPTH, D_MODEL), f),
        'router_group_w': n(ks[19], (DEPTH, D_MODEL, MOE_GROUPS), f) * D_MODEL ** -0.5,
        'router_group_b': 0.01 * n(ks[20], (DEPTH, MOE_GROUPS), f),
        'router_expert_w': n(ks[21], (DEPTH, MOE_GROUPS, D_MODEL, EXPERTS_PER_GROUP), f) * D_MODEL ** -0.5,
        'router_expert_b': 0.01 * n(ks[22], (DEPTH, MOE_GROUPS, EXPERTS_PER_GROUP), f),
        'expert_w_gate': n(ks[23], (DEPTH, N_EXPERTS, D_MODEL, D_EXPERT), f) * D_MODEL ** -0.5,
        'expert_w_up': n(ks[24], (DEPTH, N_EXPERTS, D_MODEL, D_EXPERT), f) * D_MODEL ** -0.5,
        'expert_w_down': n(ks[25], (DEPTH, N_EXPERTS, D_EXPERT, D_MODEL), f) * D_EXPERT ** -0.5,
        'ln_final': 1.0 + 0.02 * n(ks[26], (D_MODEL,), f),
    }

def reference(x_prompt, x_sample, state_conf_conv, state_ssm_conv, state_ssm,
              ln_mix, w_in, conf_dw_w, conf_dw_b, conf_ln_g, conf_ln_b,
              ssm_conv_w, ssm_conv_b, ssm_dt_bias, ssm_a_log, ssm_d, ssm_norm_g, w_out,
              ln_ffn, router_group_w, router_group_b, router_expert_w, router_expert_b,
              expert_w_gate, expert_w_up, expert_w_down, ln_final):
    bp = x_prompt.shape[0]
    xp, xs = x_prompt, x_sample
    pc, ps, ph, sc, ss, sh = [], [], [], [], [], []
    for l in range(DEPTH):
        lw = (w_in[l], conf_dw_w[l], conf_dw_b[l], conf_ln_g[l], conf_ln_b[l],
              ssm_conv_w[l], ssm_conv_b[l], ssm_dt_bias[l], ssm_a_log[l], ssm_d[l], ssm_norm_g[l], w_out[l])
        mw = (router_group_w[l], router_group_b[l], router_expert_w[l], router_expert_b[l],
              expert_w_gate[l], expert_w_up[l], expert_w_down[l])
        zc = jnp.zeros((bp, CONF_KERNEL - 1, D_CONF), xp.dtype)
        zs = jnp.zeros((bp, SSM_CONV - 1, XBC_DIM), xp.dtype)
        zh = jnp.zeros((bp, SSM_HEADS, SSM_HEAD_DIM, SSM_STATE), state_ssm.dtype)
        mp, c1, c2, c3 = mixer(rmsnorm(xp, ln_mix[l]), zc, zs, zh, *lw)
        xp = xp + mp
        xp = xp + hier_moe(rmsnorm(xp, ln_ffn[l]), *mw)
        msm, d1, d2, d3 = mixer(rmsnorm(xs, ln_mix[l]), state_conf_conv[l], state_ssm_conv[l], state_ssm[l], *lw)
        xs = xs + msm
        xs = xs + hier_moe(rmsnorm(xs, ln_ffn[l]), *mw)
        pc.append(c1); ps.append(c2); ph.append(c3)
        sc.append(d1); ss.append(d2); sh.append(d3)
    y_prompt = rmsnorm(xp, ln_final)
    y_sample = rmsnorm(xs, ln_final)
    return (y_prompt, y_sample, jnp.stack(pc), jnp.stack(ps), jnp.stack(ph),
            jnp.stack(sc), jnp.stack(ss), jnp.stack(sh))


_drawn_inputs = setup_inputs


def setup_inputs(seed=0):
    import zlib

    import numpy as np

    out = dict(_drawn_inputs(seed))
    spreads = {}
    factors = {'conf_ln_g': 12.785,
     'conf_ln_b': 12.994,
     'ssm_norm_g': 9.822,
     'router_group_b': 24.202,
     'router_expert_b': 20.039,
     'ln_final': 7.836,
     'ln_ffn': 5.954}
    for name, (base, spread) in spreads.items():
        noise = np.random.default_rng([zlib.crc32(name.encode()), seed]).standard_normal(out[name].shape)
        drawn = base * np.exp(spread * noise) if base else spread * noise
        out[name] = __import__('jax').numpy.asarray(drawn.astype(out[name].dtype))
    for name, factor in factors.items():
        out[name] = (out[name] * factor).astype(out[name].dtype)
    return out
```

```python
from contextlib import ExitStack

import concourse.bass as bass
from concourse import mybir

ALU = mybir.AluOpType
ACT = mybir.ActivationFunctionType
AX = mybir.AxisListType
F32 = mybir.dt.float32
I32 = mybir.dt.int32

P = 128
D = 1024
KD = D // P
TP = 256
NB, TB = 8, 8
TS = NB * TB
T = TP + TS
TILES = [(0, 128), (128, 128), (256, 64)]
NC = D // P
KW = 31
HIST = KW - 1
SW = 4
SH = SW - 1
H, HD, NS, G = 16, 64, 128, 2
XBC = D + 2 * G * NS
XC_N = XBC // P
C_UA, C_UB, C_Z, C_X, C_DT = 0, D, 2 * D, 3 * D, 3 * D + XBC
SEQ_W = HIST + TB
U_W = HIST + TP + NB * SEQ_W
XSEQ_W = SH + TB
X_W = SH + TP + NB * XSEQ_W
EPS = 1e-6
NE, EG, NG = 32, 8, 4
FE = 512
CAP = 64
MAXPASS = T // CAP
BIG = 8192.0

R = 6
UNIT = 4096
UNITS = ["ub0", "ua0", "ub1", "ua1", "x0", "x1", "x2", "z0", "z1", "o0", "o1", "o2", "o3"]
N_MIX = len(UNITS)

R_DWB, R_LNG, R_LNB, R_NG, N_PAR = KW, KW + 1, KW + 2, KW + 3, KW + 4


def bank_jobs():
    jobs = [(("xt", r, q), "dve") for r in range(3) for q in range(2)]
    jobs += [(("par",), "act"), (("spar",), "act")]
    jobs += [(("cst", h, q), "act") for h in range(2) for q in range(2)]
    for c in range(NC):
        jobs += [(("in", "b", c), "act"), (("in", "a", c), "act")]
    jobs += [(("in", "dt", 0), "act")]
    for c in range(XC_N):
        jobs += [(("in", "x", c), "act")]
        if c == 0:
            jobs += [(("dtT",), "act")]
        if c == 1:
            jobs += [(("ut", q), "act") for q in range(2)] + [(("us", q), "act") for q in range(2)]
    for c in range(NC):
        jobs += [(("in", "z", c), "act")]
        if c == 1:
            jobs += [(("xtail", q), "act") for q in range(3)] + [(("xs", q), "act") for q in range(3)]
    jobs += [(("mean",), "dve"), (("var",), "act")]
    for r in range(3):
        jobs += [(("xT", r, q), "dve") for q in range(2)] + [(("bT", r), "dve")]
        jobs += [(("acum", r), "dve"), (("cb", r), "dve")]
        jobs += [(("seg", r, q), "dve") for q in range(4)]
        if r > 0:
            jobs += [(("eb", r, q), "act") for q in range(2 if r < 2 else 1)]
        if r == 1:
            jobs += [(("hpT", q), "act") for q in range(2)]
        if r == 1:
            jobs += [(("yo", q), "dve") for q in range(2)]
        if r < 2:
            jobs += [(("yd", r, q), "dve") for q in range(2)]
        if r < 2:
            jobs += [(("st", r, q), "dve") for q in range(2)]
    jobs += [(("yds",), "dve")]
    for c in range(NC):
        jobs += [(("h0T", c, q), "act") for q in range(2)]
        jobs += [(("sts", c, q), "dve") for q in range(2)]
        jobs += [(("yos", c), "dve")]
    jobs += [(("rms",), "act")]
    jobs += [(("rms1",), "act")]
    jobs += [(("out", r, q), "dve") for r in range(2) for q in range(2)] + [(("outs",), "dve")]
    jobs += [(("h2", r, q), "dve") for r in range(3) for q in range(2)]
    jobs += [(("lg",), "dve"), (("rank",), "dve"), (("slots",), "dve")]
    return jobs


JOBS = bank_jobs()
J = {name: n for n, (name, _) in enumerate(JOBS)}
RANK = {}
for _who in ("act", "dve"):
    for _i, _n in enumerate([n for n, (_, who) in enumerate(JOBS) if who == _who]):
        RANK[_n] = _i


def build(nc, A, O):
    hn_dram = nc.dram_tensor("hn_scratch", (T, D), F32).ap()
    ye_dram = nc.dram_tensor("ye_scratch", (T * 4, D // 2), F32).ap()
    with ExitStack() as ctx:
        def sb(name, shape, dt=F32):
            return ctx.enter_context(nc.sbuf_tensor(name, shape, dt))

        sems = {}

        def S(name):
            if name not in sems:
                sems[name] = ctx.enter_context(nc.semaphore("s_" + name))
            return sems[name]

        bank = [ctx.enter_context(nc.psum_tensor(f"bank{i}", [P, 512], F32)) for i in range(8)]
        ring = sb("ring", [P, R, UNIT])
        xt = sb("xt", [P, 3, D])
        xtf = xt[:, :, :].rearrange("p r d -> p (r d)")
        ra = sb("region_a", [P, NC * U_W + KD * T])
        rb = sb("region_b", [P, XC_N * X_W])
        zz = sb("zz", [P, NC, T])
        vv = sb("vv", [P, NC, T])
        xc = sb("xc", [P, XC_N, T])
        yt = sb("yt", [P, NC, T])
        flat = lambda t: t[:, :, :].rearrange("p c t -> p (c t)")
        zf, vf, xcf, yf = flat(zz), flat(vv), flat(xc), flat(yt)

        ident = sb("ident", [P, P])
        tri = sb("tri", [P, P])
        later = sb("later", [P, P])
        before = sb("before", [P, P])
        trib = sb("trib", [TS, TS])
        laterb = sb("laterb", [TS, TS])
        ones = sb("ones", [P, P])
        bmask = sb("bmask", [TS, 4])
        par = sb("par", [P, NC, N_PAR])
        spar = sb("spar", [P, XC_N, SW + 1])
        lnmix = sb("lnmix", [P, KD])
        lnffn = sb("lnffn", [P, KD])
        dtb = sb("dtb", [P, H])
        alog = sb("alog", [P, H])
        dsk = sb("dsk", [P, NC])
        xs = sb("xs", [P, XC_N, TS])
        ssq = sb("ssq", [P, 8])
        rst = sb("rst", [P, 8])
        dtk = sb("dtk", [P, 3, H])
        dta = sb("dta", [P, 3, H])
        sp = sb("sp", [P, 5, 3 * H])
        na = sb("na", [P, 2 * H])
        dte = sb("dte", [P, H])

        u = ra[:, 0:NC * U_W].rearrange("p (c t) -> p c t", c=NC)
        u_seq = u[:, :, HIST + TP:].rearrange("p c (b w) -> p c b w", b=NB)
        ht = ra[:, NC * U_W:].rearrange("p (k t) -> p k t", k=KD)
        xb = rb[:, :].rearrange("p (c t) -> p c t", c=XC_N)
        xb_seq = xb[:, :, SH + TP:].rearrange("p c (b w) -> p c b w", b=NB)
        pst, sst, sstate = yf[0:N_PAR, 0:D], zf[0:SW + 1, 0:XBC], vf[0:NB * SH, 0:XBC]
        cstate = [xcf[0:4 * HIST, D * h:D * h + D] for h in range(2)]
        sig = [yf[:, D + T * b:D + T * b + T] for b in range(2)]
        uac = [yf[:, D + 2 * T + T * b:D + 2 * T + T * b + T] for b in range(1)]
        usc = vv[:, :, TP:T]
        tmp = xtf[:, 0:XC_N * TS]
        xs_rows = xtf[0:TS, 768:768 + XBC]
        wdt = xtf[:, 2304:2304 + KD * H].rearrange("p (k h) -> p k h", k=KD)
        uac.append(xtf[:, 2432:2432 + T])
        ut_rows, us_rows = xcf[0:HIST, 0:D], xcf[0:TS, D:2 * D]
        xtail_rows = yf[0:SH, 0:XBC]
        dtr = yf[0:H, 1600:1600 + T]
        xdt = rb[:, 0:3 * D].rearrange("p (r c) -> p r c", r=3)
        bt = rb[:, 3 * D:3 * D + 3 * G * NS].rearrange("p (r c) -> p r c", r=3)
        seg = ra[:, 0:H * P].rearrange("p (h i) -> p h i", h=H)
        segs = ra[0:TS, 0:H * TS].rearrange("p (h i) -> p h i", h=H)
        bm = ra[0:TS, 1024:2048].rearrange("p (b c) -> p b c", b=4)
        eb = ra[:, 2048:3072].rearrange("p (c i) -> p c i", c=NC)
        ebs = ra[:, 2048:2560].rearrange("p (c i) -> p c i", c=NC)
        hp = ra[:, 3072:4096].rearrange("p (c n) -> p c n", c=NC)
        hpt = ra[:, 4096:5120].rearrange("p (c n) -> p c n", c=NC)
        h0t = [hp, hpt]
        h0 = [ra[:, 5120:6144], ra[:, 6144:7168], xtf[:, D:2 * D], xtf[:, 2 * D:3 * D]]
        h0 = [v.rearrange("p (b n) -> p b n", b=NB) for v in h0]
        xw = xtf[:, 0:D]
        cbm = rb[:, 3840:3840 + G * P].rearrange("p (g i) -> p g i", g=G)
        rs = ra[:, 0:2 * T].rearrange("p (g t) -> p g t", g=G)
        sq = rb[:, 0:NC * T].rearrange("p (c t) -> p c t", c=NC)
        h2t = ra[:, 0:KD * T].rearrange("p (k t) -> p k t", k=KD)
        hn = xcf[:, 0:3 * D].rearrange("p (r d) -> p r d", r=3)
        gat = [rb[0:CAP, D * b:D * b + D] for b in range(2)]
        xgt = [ra[:, 2560 + 512 * b:3072 + 512 * b].rearrange("p (k s) -> p k s", k=KD) for b in range(2)]
        hidt = [ra[:, 3584 + 256 * b:3840 + 256 * b].rearrange("p (k s) -> p k s", k=4) for b in range(2)]
        sil = [zf[0:CAP, 512 * b:512 * b + 512] for b in range(2)]
        hid = [zf[0:CAP, 1024 + 512 * b:1536 + 512 * b] for b in range(2)]
        yo = [yf[:, 512 * b:512 * b + 512] for b in range(2)]
        wr = zf[:, 2048:2048 + KD * 36].rearrange("p (k n) -> p k n", k=KD)
        rbias = zf[:, 2336:2372]
        gfin = vf[:, 0:D]
        at = [4096]

        def moe(n):
            at[0] += n
            assert at[0] <= NC * U_W + KD * T
            return ra[:, at[0] - n:at[0]]

        r3 = lambda t: t.rearrange("p (r n) -> p r n", r=3)
        lg = r3(moe(3 * 36))
        e1, e2, aa, pos = (r3(moe(3 * NE)) for _ in range(4))
        og, sg4, t4 = (r3(moe(3 * NG)) for _ in range(3))
        le, o1, o2, s8, t8 = (r3(moe(3 * EG)) for _ in range(5))
        t32 = r3(moe(3 * NE))
        cols = moe(3 * 16).rearrange("p (n r) -> p n r", r=3)
        val = [moe(3 * 3 * NE).rearrange("p (r c e) -> p r c e", r=3, c=3) for _ in range(2)]
        osel = moe(3 * 2 * P).rearrange("p (r w s) -> p r w s", r=3, w=2)
        slotno = moe(P)
        desc4, desc8, tokid, halfrow = moe(NG), moe(EG), moe(3), moe(1)
        cnt, wsl = moe(NE), moe(NE + 1)
        gidx = moe(NE + 1).bitcast(I32)
        sidx = moe(NE + 1).bitcast(I32)
        gcur = [moe(1).bitcast(I32) for _ in range(2)]
        scur = [moe(1).bitcast(I32) for _ in range(2)]
        mcount = moe(1).bitcast(I32)
        wait_word = moe(6)
        M_SSUM, M_G1, M_M1, M_M2, M_E, M_R, M_W1, M_W2, M_S1, M_S2, M_T = range(11)

        def toks(r):
            return slice(TILES[r][0], TILES[r][0] + TILES[r][1])

        def bc(ap, shape):
            return ap.to_broadcast(shape)

        def wait(eng, sem, value):
            if isinstance(value, int) and value <= 0:
                return
            eng.wait_ge(sem, value)

        def wait_apart(eng, sem, value):
            eng.wait_ge(S("ident"), 1)
            eng.wait_ge(sem, value)

        filled = S("filled")
        free = {"act": S("act_read"), "dve": S("dve_read")}

        def take(pe, *name):
            n = J[name]
            if n >= 8:
                pe.wait_ge(free[JOBS[n - 8][1]], RANK[n - 8] + 1)
            return bank[n % 8]

        def got(eng, *name):
            eng.wait_ge(filled, J[name] + 1)
            return bank[J[name] % 8]

        def read_of(name):
            n = J[name]
            return free[JOBS[n][1]], RANK[n] + 1

        def after_read(eng, *name):
            eng.wait_ge(*read_of(name))

        ring_in = [S(f"ring_in{s}") for s in range(R)]

        def landed(eng, unit):
            n = UNITS.index(unit)
            eng.wait_ge(ring_in[n % R], 16 * (n // R + 1))
            return ring[:, n % R, :]

        slot_pre = [len([n for n in range(N_MIX) if n % R == s]) for s in range(R)]
        u_slot = [(N_MIX + m) % R for m in range(R)]
        ctx.enter_context(nc.allow_non_contiguous_dma(reason="small parameters and state rows"))
        block = ctx.enter_context(nc.Block())
        w_in = A["w_in"][0].rearrange("(p k) c -> p k c", k=KD)
        w_out = A["w_out"][0].rearrange("(c p) n -> p c n", p=P)

        def expert_src(m, e):
            w = [A["expert_w_gate"], A["expert_w_up"], A["expert_w_down"]][m % 3]
            v = w[0, bass.ds(e, 1)].rearrange("e a b -> (e a) b")
            return v.rearrange("(p k) f -> p (k f)", p=P)

        @block.sync
        def _(sp_):
            for r, (t0, n) in enumerate(TILES):
                src = A["x_prompt"][0, t0:t0 + n, :] if r < 2 else A["x_sample"].rearrange("b t d -> (b t) d")
                sp_.dma_start(xt[0:n, r, :], src).then_inc(S("x_in"), 16)
            last = {"ub0": ("in", "a", 3), "ua0": ("in", "a", 3), "ub1": ("in", "a", 7), "ua1": ("in", "a", 7),
                    "x0": ("in", "x", 3), "x1": ("in", "x", 7), "x2": ("in", "x", 11),
                    "z0": ("in", "z", 3), "z1": ("in", "z", 7)}
            col = {"ub": C_UB, "ua": C_UA, "x": C_X, "z": C_Z}

            def slot_free(n):
                if n >= R:
                    old = UNITS[n - R]
                    if old == "o3":
                        sp_.wait_ge(filled, J[("outs",)] + 1)
                    elif old[0] == "o":
                        sp_.wait_ge(S("wo_used"), int(old[1]) + 1)
                    else:
                        sp_.wait_ge(filled, J[last[old]] + 1)

            for n, unit in enumerate(UNITS):
                slot_free(n)
                kind, i = unit[:-1], int(unit[-1])
                if kind == "o":
                    dst, src = ring[:, n % R, :].rearrange("p (c n) -> p c n", c=4), w_out[:, 4 * i:4 * i + 4, :]
                else:
                    c0 = col[kind] + 512 * i
                    dst, src = ring[:, n % R, :].rearrange("p (k c) -> p k c", k=KD), w_in[:, :, c0:c0 + 512]
                sp_.dma_start(dst, src).then_inc(ring_in[n % R], 16)
            for m in range(R):
                slot_free(N_MIX + m)
                sp_.dma_start(ring[:, u_slot[m], :], expert_src(m, m // 3)).then_inc(ring_in[u_slot[m]], 16)
            with sp_.Fori(1, NE // 2) as i:
                for m in range(R):
                    b = m // 3
                    sp_.wait_ge(S("gu_done") if m % 3 < 2 else S("dn_done"), 2 * i + b - 1)
                    sp_.dma_start(ring[:, u_slot[m], :], expert_src(m, 2 * i + b)).then_inc(ring_in[u_slot[m]], 16)
            sp_.wait_ge(S("count_ready"), 1)
            over = sp_.value_load(mcount[0:1, 0:1], min_val=0, max_val=T)
            with sp_.If(over > CAP):
                sp_.wait_ge(S("dn_done"), NE)
                with sp_.Fori(0, MAXPASS - 1) as q:
                    with sp_.Fori(0, NE) as e:
                        sp_.wait_ge(S("sl_next"), q * NE + e + 1)
                        for m in range(3):
                            sp_.dma_start(ring[:, m, :], expert_src(m, e)).then_inc(S("sl_w"), 16)
            sp_.wait_ge(S("ye_all"), 1)
            sp_.wait_ge(S("dn_done"), NE)
            ye_tok = ye_dram.rearrange("(t c) n -> t (c n)", c=4)
            for r, (t0, n) in enumerate(TILES):
                sp_.dma_start(ring[0:n, r, 0:2 * D], ye_tok[t0:t0 + n, :]).then_inc(S("ye_in"), 16)
            for r, (t0, n) in enumerate(TILES):
                sp_.wait_ge(S("y_final"), r + 1)
                dst = O["y_prompt"][0, t0:t0 + n, :] if r < 2 else O["y_sample"].rearrange("b t d -> (b t) d")
                sp_.dma_start(dst, xt[0:n, r, :]).then_inc(S("y_out"), 16)
            sp_.wait_ge(S("y_out"), 48)

        @block.gpsimd
        def _(pool):
            own = [0]

            def link(ins):
                own[0] += 1
                ins.then_inc(S("pool_own"), 1)
                pool.wait_ge(S("pool_own"), own[0])

            pool.memset(rst[:, :], 1.0)
            link(pool.memset(ssq[:, :], 0.0))
            pool.memset(ssq[:, 7:8], EPS).then_inc(S("eps"), 1)
            for m in (ident, before, later):
                pool.memset(m[:, :], 0.0)
            for m in (tri, ones, trib, laterb, bmask):
                pool.memset(m[:, :], 1.0)
            pool.memset(u[:, :, 0:HIST], 0.0)
            link(pool.memset(xb[:, :, 0:SH], 0.0))
            sel = lambda o, pat, op, fill, base, cm: pool.affine_select(
                out=o, in_=o, compare_op=op, fill=fill, base=base, pattern=pat, channel_multiplier=cm)
            sel(ident[:, :], [[-1, P]], ALU.not_equal, 1.0, 0, 1).then_inc(S("ident"), 1)
            sel(tri[:, :], [[1, P]], ALU.is_ge, 0.0, 0, -1)
            sel(later[:, :], [[1, P]], ALU.is_ge, 1.0, 0, -1)
            sel(before[:, :], [[-1, P]], ALU.is_ge, 1.0, 0, 1)
            sel(trib[:, :], [[1, TS]], ALU.is_ge, 0.0, 0, -1)
            link(sel(laterb[:, :], [[-1, TS]], ALU.is_gt, 0.0, 0, 1))
            for m in (trib, laterb):
                v = m[:, :].rearrange("p (b i) -> p b i", b=NB)
                link(sel(v, [[-TB, NB], [0, TB]], ALU.is_ge, 0.0, 0, 1))
                link(sel(v, [[TB, NB], [0, TB]], ALU.is_ge, 0.0, TB - 1, -1))
            for half in range(2):
                v = bmask[32 * half:32 * half + 32, :]
                link(sel(v, [[-TB, 4]], ALU.is_ge, 0.0, 0, 1))
                link(sel(v, [[TB, 4]], ALU.is_ge, 0.0, TB - 1, -1))
            pool.memset(dtk[:, :, :], 0.0).then_inc(S("consts"), 1)

            for c in range(NC):
                b = c % 2
                after_read(pool, "in", "a", c)
                pool.tensor_tensor(u[:, c, HIST:HIST + TP], uac[b][:, 0:TP], sig[b][:, 0:TP], ALU.mult)
                link(pool.tensor_tensor(usc[:, c, :], uac[b][:, TP:T], sig[b][:, TP:T], ALU.mult))
                pool.tensor_copy(u_seq[:, c, :, HIST:], usc[:, c, :].rearrange("p (b t) -> p b t", b=NB))\
                    .then_inc(S("glu"), 1)
            pool.wait_ge(S("glu"), NC)
            pool.wait_ge(*read_of(("cst", 1, 1)))
            w4 = lambda w, k, n: bc(w[:, :, k:k + 1].unsqueeze(3), [P, n, NB, TB])
            acc = vv[:, :, TP:T].rearrange("p c (b t) -> p c b t", b=NB)
            tmp4 = tmp[:, 0:NC * TS].rearrange("p (c b t) -> p c b t", c=NC, b=NB)
            pool.wait_ge(filled, J[("us", 1)] + 1)
            link(pool.tensor_tensor(acc, u_seq[:, :, :, 0:TB], w4(par, 0, NC), ALU.mult))
            link(pool.tensor_tensor(acc, acc, w4(par, R_DWB, NC), ALU.add))
            for k in range(1, KW):
                link(pool.tensor_tensor(tmp4, u_seq[:, :, :, k:k + TB], w4(par, k, NC), ALU.mult))
                ins = pool.tensor_tensor(acc, acc, tmp4, ALU.add)
                if k < KW - 1:
                    link(ins)
                else:
                    ins.then_inc(S("conv_s"), 1)
            pool.wait_ge(S("conv_s"), 1)
            after_read(pool, "in", "x", XC_N - 1)
            link(pool.tensor_copy(xb_seq[:, :, :, SH:], xs[:, :, :].rearrange("p c (b t) -> p c b t", b=NB)))
            acc = xc[:, :, TP:T].rearrange("p c (b t) -> p c b t", b=NB)
            tmp4 = tmp.rearrange("p (c b t) -> p c b t", c=XC_N, b=NB)
            pool.wait_ge(S("u_out"), 16 * (1 + NB))
            link(pool.tensor_tensor(acc, xb_seq[:, :, :, 0:TB], w4(spar, 0, XC_N), ALU.mult))
            link(pool.tensor_tensor(acc, acc, w4(spar, SW, XC_N), ALU.add))
            for k in range(1, SW):
                link(pool.tensor_tensor(tmp4, xb_seq[:, :, :, k:k + TB], w4(spar, k, XC_N), ALU.mult))
                ins = pool.tensor_tensor(acc, acc, tmp4, ALU.add)
                if k < SW - 1:
                    link(ins)
                else:
                    ins.then_inc(S("xconv_s"), 1)
            pool.wait_ge(S("xconv_s"), 1)

            def h0_load(c):
                for b in range(NB):
                    pool.dma_start(h0[c % 4][:, b, :], A["state_ssm"][0, b, 2 * c:2 * c + 2].rearrange(
                        "h p n -> (h p) n")).then_inc(S(f"h0_in{c % 4}"), 16)

            pool.wait_ge(S("conv"), NC)
            pool.wait_ge(filled, J[("in", "z", NC - 1)] + 1)
            for c in range(2):
                h0_load(c)
            pool.wait_ge(S("x_out"), 16 * (1 + SH))
            for c in range(2, 4):
                h0_load(c)
            pool.wait_ge(S("hp_done"), 1)
            pool.dma_start(O["new_ssm_prompt"][0, 0].rearrange("(c h) p n -> (h p) c n", c=NC), hp)\
                .then_inc(S("hp_out"), 16)
            for c in range(NC):
                pool.wait_ge(S("h0_new"), c + 1)
                for b in range(NB):
                    pool.dma_start(O["new_ssm_sample"][0, b, 2 * c:2 * c + 2].rearrange("h p n -> (h p) n"),
                                   h0[c % 4][:, b, :]).then_inc(S(f"h0_out{c % 4}"), 16)
                if c + 4 < NC:
                    pool.wait_ge(S(f"h0_out{c % 4}"), 16 * NB)
                    h0_load(c + 4)

            for k in range(2, 4):
                pool.wait_ge(S(f"h0_out{k}"), 2 * 16 * NB)
            pool.wait_ge(filled, J[("sts", NC - 1, 1)] + 1)
            for r, (t0, n) in enumerate(TILES):
                src = A["x_prompt"][0, t0:t0 + n, :] if r < 2 else A["x_sample"].rearrange("b t d -> (b t) d")
                pool.dma_start(xt[0:n, r, :], src).then_inc(S("x_again"), 16)
            pool.wait_ge(S("gated"), 1)
            pool.dma_start(wr[:, :, 0:NG], A["router_group_w"][0].rearrange("(p k) n -> p k n", k=KD))\
                .then_inc(S("wr_in"), 16)
            for g in range(NG):
                pool.dma_start(wr[:, :, NG + EG * g:NG + EG * g + EG],
                               A["router_expert_w"][0, g].rearrange("(p k) n -> p k n", k=KD))\
                    .then_inc(S("wr_in"), 16)
            pool.dma_start(rbias[:, 0:NG], A["router_group_b"].to_broadcast([P, NG])).then_inc(S("wr_in"), 16)
            pool.dma_start(rbias[:, NG:], A["router_expert_b"].rearrange("a g e -> a (g e)").to_broadcast([P, NE]))\
                .then_inc(S("wr_in"), 16)

            pool.wait_ge(S("y_done"), 1)
            pool.iota(slotno[:, :].rearrange("p (a s) -> p a s", a=2), [[0, 2], [1, CAP]], base=0,
                      channel_multiplier=0, allow_small_or_imprecise_dtypes=True)
            pool.iota(desc4, [[-1, NG]], base=NG, channel_multiplier=0, allow_small_or_imprecise_dtypes=True)
            pool.iota(desc8, [[-1, EG]], base=EG, channel_multiplier=0, allow_small_or_imprecise_dtypes=True)
            pool.iota(tokid, [[P, 3]], base=0, channel_multiplier=1, allow_small_or_imprecise_dtypes=True)
            link(pool.memset(halfrow, 2 * BIG))
            link(pool.memset(halfrow[CAP:P, :], 2 * BIG + 1))
            pool.memset(gidx, int(BIG))
            for b in range(2):
                pool.memset(gat[b], 0.0)
            pool.memset(sidx, int(2 * BIG)).then_inc(S("rconst"), 1)

            pool.wait_ge(S("hn_out"), 48)
            pool.wait_ge(S("idx"), 1)

            def carry_wait(w):
                pool.tensor_tensor(wait_word[:, w:w + 1], halfrow, halfrow, ALU.add)

            def gather_dma(b):
                pool.indirect_dma_start(gat[b], None, hn_dram[:, :],
                                        bass.IndirectOffsetOnAxis(ap=gcur[b][0:CAP, 0:1], axis=0),
                                        bounds_check=T - 1, oob_is_err=False).then_inc(S(f"gath{b}"), 16)

            def scatter_dma(b, sem):
                pool.indirect_dma_start(ye_dram[:, :], bass.IndirectOffsetOnAxis(ap=scur[b][:, 0:1], axis=0),
                                        yo[b], None, bounds_check=4 * T - 1, oob_is_err=False)\
                    .then_inc(sem, 16)

            pool.tensor_copy(gcur[0], gidx[:, 0:1]).then_inc(S("cur"), 1)
            pool.wait_ge(S("cur"), 1)
            gather_dma(0)

            def expert(i, b):
                e = 2 * i + b
                wait(pool, S("xg_T"), e)
                pool.tensor_copy(gcur[1 - b], gidx[:, bass.ds(e + 1, 1)])
                wait(pool, S(f"scat{b}"), 16 * i)
                pool.tensor_copy(scur[b], sidx[:, bass.ds(e, 1)]).then_inc(S("cur"), 1)
                pool.wait_ge(S("cur"), e + 2)
                carry_wait(0)
                gather_dma(1 - b)
                pool.wait_ge(S("yo"), e + 1)
                carry_wait(1)
                scatter_dma(b, S(f"scat{b}"))

            for b in range(2):
                expert(0, b)
            with pool.Fori(1, NE // 2) as i:
                for b in range(2):
                    expert(i, b)
            pool.wait_ge(S("gath0"), 16 * (NE // 2 + 1))
            for b in range(2):
                pool.wait_ge(S(f"scat{b}"), 16 * NE // 2)
            over = pool.value_load(mcount[0:1, 0:1], min_val=0, max_val=T)
            with pool.If(over > CAP):
                pool.memset(gat[0], 0.0).then_inc(S("sl_next"), 1)
                with pool.Fori(0, MAXPASS - 1) as q:
                    pool.wait_ge(S("sl_idx"), q + 1)
                    carry_wait(2)
                    with pool.Fori(0, NE) as e:
                        n = q * NE + e
                        pool.tensor_copy(gcur[0], gidx[:, bass.ds(e, 1)]).then_inc(S("sl_cur"), 1)
                        pool.tensor_copy(scur[0], sidx[:, bass.ds(e, 1)]).then_inc(S("sl_cur"), 1)
                        pool.wait_ge(S("sl_cur"), 2 * n + 2)
                        carry_wait(3)
                        pool.indirect_dma_start(gat[0], None, hn_dram[:, :],
                                                bass.IndirectOffsetOnAxis(ap=gcur[0][0:CAP, 0:1], axis=0),
                                                bounds_check=T - 1, oob_is_err=False).then_inc(S("sl_g"), 16)
                        pool.wait_ge(S("sl_y"), n + 1)
                        carry_wait(4)
                        scatter_dma(0, S("sl_sc"))
                        pool.wait_ge(S("sl_sc"), 16 * (n + 1))
                        carry_wait(5)
                        pool.memset(gcur[1], 0).then_inc(S("sl_next"), 1)
            pool.memset(gat[0], 0.0).then_inc(S("ye_all"), 1)
            pool.wait_ge(S("hp_out"), 16)
            for k in range(4):
                pool.wait_ge(S(f"h0_out{k}"), 2 * 16 * NB)

        @block.tensor
        def _(pe):
            pe.wait_ge(S("ident"), 1)
            for r, (t0, n) in enumerate(TILES):
                pe.wait_ge(S("xn"), r + 1)
                for q in range(2):
                    pt = take(pe, "xt", r, q)
                    for k in range(4):
                        ins = pe.transpose(pt[:, P * k:P * k + n], xt[0:n, r, 4 * q + k:D:KD], ident[0:n, 0:n])
                    ins.then_inc(filled, 1)
            pe.wait_ge(S("par_in"), 16 * 11)
            pt = take(pe, "par")
            for c in range(NC):
                ins = pe.transpose(pt[:, N_PAR * c:N_PAR * (c + 1)], pst[:, P * c:P * c + P],
                                   ident[0:N_PAR, 0:N_PAR])
            ins.then_inc(filled, 1)
            pt = take(pe, "spar")
            for c in range(XC_N):
                pe.transpose(pt[:, 5 * c:5 * c + 5], sst[:, P * c:P * c + P], ident[0:5, 0:5])
                ins = pe.transpose(pt[:, 60 + 24 * c:84 + 24 * c], sstate[:, P * c:P * c + P], ident[0:24, 0:24])
            ins.then_inc(filled, 1)
            for h in range(2):
                for q in range(2):
                    pt = take(pe, "cst", h, q)
                    for c in range(4):
                        cc = 4 * q + c
                        ins = pe.transpose(pt[:, 120 * c:120 * c + 120], cstate[h][:, P * cc:P * cc + P],
                                           ident[0:120, 0:120])
                    ins.then_inc(filled, 1)

            pe.wait_ge(*read_of(("xt", 2, 1)))

            def project(name, unit, c):
                pt = take(pe, *name)
                if unit is None:
                    w, m = wdt, H
                else:
                    w, m = landed(pe, unit).rearrange("p (k c) -> p k c", k=KD)[:, :, P * c:P * c + P], P
                for k in range(KD):
                    ins = pe.matmul(pt[0:m, 0:T], w[:, k, :], ht[:, k, :], start=k == 0, stop=k == KD - 1)
                ins.then_inc(filled, 1)

            for c in range(NC):
                project(("in", "b", c), f"ub{c // 4}", c % 4)
                project(("in", "a", c), f"ua{c // 4}", c % 4)
            pe.wait_ge(S("wdt_in"), 16)
            project(("in", "dt", 0), None, 0)
            for c in range(XC_N):
                project(("in", "x", c), f"x{c // 4}", c % 4)
                if c == 0:
                    after_read(pe, "in", "dt", 0)
                    pt = take(pe, "dtT")
                    for r, (t0, n) in enumerate(TILES):
                        ins = pe.transpose(pt[0:n, H * r:H * r + H], dtr[:, t0:t0 + n], ident[0:H, 0:H])
                    ins.then_inc(filled, 1)
                if c == 1:
                    pe.wait_ge(S("glu"), NC)
                    for q in range(2):
                        pt = take(pe, "ut", q)
                        for k in range(4):
                            ins = pe.transpose(pt[0:HIST, P * k:P * k + P], u[:, 4 * q + k, TP:TP + HIST],
                                               ident[:, :])
                        ins.then_inc(filled, 1)
                    for q in range(2):
                        pt = take(pe, "us", q)
                        for k in range(4):
                            ins = pe.transpose(pt[0:TS, P * k:P * k + P], usc[:, 4 * q + k, :], ident[:, :])
                        ins.then_inc(filled, 1)
            for c in range(NC):
                project(("in", "z", c), f"z{c // 4}", c % 4)
                if c == 1:
                    after_read(pe, "in", "x", XC_N - 1)
                    for q in range(3):
                        pt = take(pe, "xtail", q)
                        for k in range(4):
                            ins = pe.transpose(pt[0:SH, P * k:P * k + P], xb[:, 4 * q + k, TP:TP + SH], ident[:, :])
                        ins.then_inc(filled, 1)
                    for q in range(3):
                        pt = take(pe, "xs", q)
                        for k in range(4):
                            ins = pe.transpose(pt[0:TS, P * k:P * k + P], xs[:, 4 * q + k, :], ident[:, :])
                        ins.then_inc(filled, 1)

            pe.wait_ge(S("conv"), NC)
            pe.wait_ge(S("conv_s"), 1)
            pt = take(pe, "mean")
            for c in range(NC):
                ins = pe.matmul(pt[:, 0:T], ones[:, :], vv[:, c, :], start=c == 0, stop=c == NC - 1)
            ins.then_inc(filled, 1)
            pe.wait_ge(S("vsq"), 1)
            pt = take(pe, "var")
            for c in range(NC):
                ins = pe.matmul(pt[:, 0:T], ones[:, :], yt[:, c, :], start=c == 0, stop=c == NC - 1)
            ins.then_inc(filled, 1)

            pe.wait_ge(S("xact"), 1)
            for r, (t0, n) in enumerate(TILES):
                m_tri, m_later = (tri, later) if r < 2 else (trib, laterb)
                tt = toks(r)
                for q in range(2):
                    pt = take(pe, "xT", r, q)
                    for k in range(4):
                        ins = pe.transpose(pt[0:n, P * k:P * k + P], xc[:, 4 * q + k, tt], ident[:, :])
                    ins.then_inc(filled, 1)
                pt = take(pe, "bT", r)
                for g in range(G):
                    ins = pe.transpose(pt[0:n, P * g:P * g + P], xc[:, NC + g, tt], ident[:, :])
                ins.then_inc(filled, 1)
                pe.wait_ge(S("dta"), 1)
                pt = take(pe, "acum", r)
                pe.matmul(pt[0:n, 0:H], m_tri[0:n, 0:n], dta[0:n, r, :], start=True, stop=True)
                pe.matmul(pt[0:n, H:2 * H], m_later[0:n, 0:n], dta[0:n, r, :], start=True, stop=True)\
                    .then_inc(filled, 1)
                pt = take(pe, "cb", r)
                for g in range(G):
                    ins = pe.matmul(pt[0:n, P * g:P * g + n], xc[:, NC + g, tt], xc[:, NC + G + g, tt],
                                    start=True, stop=True)
                ins.then_inc(filled, 1)
                for q in range(4):
                    pt = take(pe, "seg", r, q)
                    for k in range(4):
                        ins = pe.matmul(pt[0:n, n * k:n * k + n], bc(dta[0:n, r, 4 * q + k:4 * q + k + 1], [n, n]),
                                        m_tri[0:n, 0:n], start=True, stop=True)
                    ins.then_inc(filled, 1)
                if r > 0:
                    per = 4 if r < 2 else 8
                    for q in range(NC // per):
                        pt = take(pe, "eb", r, q)
                        for k in range(per):
                            for hh in range(2):
                                hd = 2 * (per * q + k) + hh
                                ins = pe.matmul(pt[64 * hh:64 * hh + 64, n * k:n * k + n],
                                                bc(dta[0:n, r, hd:hd + 1], [n, HD]), m_tri[0:n, 0:n],
                                                start=True, stop=True)
                        ins.then_inc(filled, 1)
                if r == 1:
                    after_read(pe, "st", 0, 1)
                    for q in range(2):
                        pt = take(pe, "hpT", q)
                        for k in range(4):
                            ins = pe.transpose(pt[:, P * k:P * k + P], hp[:, 4 * q + k, :], ident[:, :])
                        ins.then_inc(filled, 1)
                    after_read(pe, "hpT", 1)
                    for q in range(2):
                        pt = take(pe, "yo", q)
                        for k in range(4):
                            ins = pe.matmul(pt[:, P * k:P * k + P], hpt[:, 4 * q + k, :],
                                            xc[:, NC + G + q, tt], start=True, stop=True)
                        ins.then_inc(filled, 1)
                pe.wait_ge(S("mdone"), r + 1)
                if r < 2:
                    for q in range(2):
                        pt = take(pe, "yd", r, q)
                        for k in range(4):
                            for hh in range(2):
                                hd = 2 * (4 * q + k) + hh
                                ins = pe.matmul(pt[64 * hh:64 * hh + 64, P * k:P * k + P],
                                                xdt[:, r, HD * hd:HD * hd + HD], seg[:, hd, :],
                                                start=True, stop=True)
                        ins.then_inc(filled, 1)
                    pe.wait_ge(S("xw"), r + 1)
                    for q in range(2):
                        pt = take(pe, "st", r, q)
                        for k in range(4):
                            c = 4 * q + k
                            ins = pe.matmul(pt[:, P * k:P * k + P], xw[:, P * c:P * c + P],
                                            bt[:, r, NS * q:NS * q + NS], start=True, stop=True)
                        ins.then_inc(filled, 1)
            pt = take(pe, "yds")
            for k in range(NC):
                for hh in range(2):
                    hd = 2 * k + hh
                    ins = pe.matmul(pt[64 * hh:64 * hh + 64, TS * k:TS * k + TS],
                                    xdt[0:TS, 2, HD * hd:HD * hd + HD], segs[:, hd, :], start=True, stop=True)
            ins.then_inc(filled, 1)
            pe.wait_ge(S("xw"), 3)
            pe.wait_ge(S("bm"), 1)
            for c in range(NC):
                g = c // 4
                pe.wait_ge(S(f"h0_in{c % 4}"), 16 * NB * (c // 4 + 1))
                for q in range(2):
                    pt = take(pe, "h0T", c, q)
                    for k in range(4):
                        ins = pe.transpose(pt[:, P * k:P * k + P], h0[c % 4][:, 4 * q + k, :], ident[:, :])
                    ins.then_inc(filled, 1)
                for q in range(2):
                    pt = take(pe, "sts", c, q)
                    pe.matmul(pt[:, :].rearrange("p (b n) -> p b n", b=4),
                              xw[32 * q:32 * q + 32, P * c:P * c + P],
                              bm[32 * q:32 * q + 32, :, NS * g:NS * g + NS], start=True, stop=True)\
                        .then_inc(filled, 1)
                after_read(pe, "h0T", c, 1)
                pt = take(pe, "yos", c)
                for b in range(NB):
                    ins = pe.matmul(pt[:, TB * b:TB * b + TB], h0t[c % 2][:, b, :],
                                    xc[:, NC + G + g, TP + TB * b:TP + TB * b + TB], start=True, stop=True)
                ins.then_inc(filled, 1)

            pe.wait_ge(S("ysq"), 1)
            for g, name in enumerate(("rms", "rms1")):
                pt = take(pe, name)
                for k in range(4):
                    ins = pe.matmul(pt[:, 0:T], ones[:, :], sq[:, 4 * g + k, :], start=k == 0, stop=k == 3)
                ins.then_inc(filled, 1)

            ob = [take(pe, "out", r, q) for r in range(2) for q in range(2)] + [take(pe, "outs")]
            for c in range(2 * NC):
                w = landed(pe, f"o{c // 4}").rearrange("p (c n) -> p c n", c=4)[:, c % 4, :]
                if c == 0:
                    pe.wait_ge(S("v_done"), 1)
                if c == NC:
                    pe.wait_ge(S("y_done"), 1)
                mix = vv[:, c, :] if c < NC else yt[:, c - NC, :]
                last = c == 2 * NC - 1
                for r in range(2):
                    for q in range(2):
                        ins = pe.matmul(ob[2 * r + q][:, :], mix[:, toks(r)], w[:, 512 * q:512 * q + 512],
                                        start=c == 0, stop=last)
                        if last:
                            ins.then_inc(filled, 1)
                for q in range(2):
                    ins = pe.matmul(ob[4][64 * q:64 * q + 64, :], mix[:, toks(2)], w[:, 512 * q:512 * q + 512],
                                    start=c == 0, stop=last)
                if last:
                    ins.then_inc(filled, 1)
                elif c % 4 == 3:
                    ins.then_inc(S("wo_used"), 1)

            for r, (t0, n) in enumerate(TILES):
                pe.wait_ge(S("hn"), r + 1)
                for q in range(2):
                    pt = take(pe, "h2", r, q)
                    for k in range(4):
                        ins = pe.transpose(pt[:, P * k:P * k + n], hn[0:n, r, 4 * q + k:D:KD], ident[0:n, 0:n])
                    ins.then_inc(filled, 1)
            pe.wait_ge(S("wr_in"), 16 * 7)
            after_read(pe, "h2", 2, 1)
            pt = take(pe, "lg")
            for r, (t0, n) in enumerate(TILES):
                for k in range(KD):
                    ins = pe.matmul(pt[0:n, 36 * r:36 * r + 36], h2t[:, k, t0:t0 + n], wr[:, k, :],
                                    start=k == 0, stop=k == KD - 1)
            ins.then_inc(filled, 1)
            pe.wait_ge(S("chosen"), 1)
            pt = take(pe, "rank")
            for r in range(4):
                for rr in range(min(r, 2) + 1):
                    m = before if rr == r else ones
                    ins = pe.matmul(pt[:, NE * r:NE * r + NE], m[:, :], aa[:, rr, :],
                                    start=rr == 0, stop=rr == min(r, 2))
            ins.then_inc(filled, 1)

            def slot_values(pt):
                for n_, (r, w) in enumerate([(r, w) for r in range(3) for w in range(2)]):
                    n = TILES[r][1]
                    ins = pe.matmul(pt[:, 0:3 * NE], osel[0:n, r, w, :],
                                    val[w][0:n, r, :, :].rearrange("p c e -> p (c e)"), start=n_ == 0, stop=n_ == 5)
                return ins

            pe.wait_ge(S("osel"), 1)
            slot_values(take(pe, "slots")).then_inc(filled, 1)
            after_read(pe, "slots")
            pe.wait_ge(free["act"], len([1 for _, who in JOBS if who == "act"]))

            def tokens_T(b):
                for k in range(KD):
                    ins = pe.transpose(bank[2 + b][:, CAP * k:CAP * k + CAP], gat[b][:, k:D:KD], ident[0:CAP, 0:CAP])
                return ins

            def carry_wait(b):
                pe.transpose(bank[2 + b][:, 0:P], ident[:, :], ident[:, :])

            def gate_up(b, wg, wu):
                for k in range(KD):
                    st = dict(start=k == 0, stop=k == KD - 1)
                    pe.matmul(bank[b][0:CAP, :], xgt[b][:, k, :], wg[:, FE * k:FE * k + FE], **st)
                    ins = pe.matmul(bank[b][CAP:P, :], xgt[b][:, k, :], wu[:, FE * k:FE * k + FE], **st)
                return ins

            def hidden_T(b):
                for k in range(4):
                    ins = pe.transpose(bank[4 + b][:, CAP * k:CAP * k + CAP], hid[b][:, k:FE:4], ident[0:CAP, 0:CAP])
                return ins

            def down(b, wd):
                for k in range(4):
                    for q in range(2):
                        ins = pe.matmul(bank[6 + b][CAP * q:CAP * q + CAP, :], hidt[b][:, k, :],
                                        wd[:, D * k + 512 * q:D * k + 512 * q + 512], start=k == 0, stop=k == 3)
                return ins

            pe.wait_ge(S("gath0"), 16)
            tokens_T(0).then_inc(S("xg_T"), 1)

            def expert(i, b):
                e = 2 * i + b
                m = [u_slot[3 * b + j] for j in range(3)]
                for j in range(2):
                    pe.wait_ge(ring_in[m[j]], 16 * (slot_pre[m[j]] + 1) + 16 * i)
                pe.wait_ge(S("xgt"), e + 1)
                wait(pe, S("hid"), e - 1)
                gate_up(b, ring[:, m[0], :], ring[:, m[1], :]).then_inc(S("gu_done"), 1)
                pe.wait_ge(S(f"gath{1 - b}"), 16 * (i + 1 + b))
                wait(pe, S("xgt"), e)
                carry_wait(1 - b)
                tokens_T(1 - b).then_inc(S("xg_T"), 1)
                wait_apart(pe, S("hid"), e + 1)
                wait(pe, S("hidt"), e - 1)
                hidden_T(b).then_inc(S("hid_T"), 1)
                pe.wait_ge(ring_in[m[2]], 16 * (slot_pre[m[2]] + 1) + 16 * i)
                pe.wait_ge(S("hidt"), e + 1)
                wait(pe, S("yo"), e - 1)
                down(b, ring[:, m[2], :]).then_inc(S("dn_done"), 1)

            for b in range(2):
                expert(0, b)
            with pe.Fori(1, NE // 2) as i:
                for b in range(2):
                    expert(i, b)
            over = pe.value_load(mcount[0:1, 0:1], min_val=0, max_val=T)
            with pe.If(over > CAP):
                pe.wait_ge(S("xgt"), NE + 1)
                pe.wait_ge(S("yo"), NE)
                with pe.Fori(0, MAXPASS - 1) as q:
                    pe.wait_ge(S("sl_osel"), q + 1)
                    slot_values(bank[0]).then_inc(S("sl_slots"), 1)
                    wait_apart(pe, S("sl_idx"), q + 1)
                    with pe.Fori(0, NE) as e:
                        n = q * NE + e
                        pe.wait_ge(S("sl_g"), 16 * (n + 1))
                        carry_wait(0)
                        tokens_T(0).then_inc(S("sl_xT"), 1)
                        pe.wait_ge(S("sl_x"), n + 1)
                        pe.wait_ge(S("sl_w"), 48 * (n + 1))
                        gate_up(0, ring[:, 0, :], ring[:, 1, :]).then_inc(S("sl_gu"), 1)
                        wait_apart(pe, S("sl_hid"), n + 1)
                        hidden_T(0).then_inc(S("sl_hT"), 1)
                        pe.wait_ge(S("sl_hidt"), n + 1)
                        down(0, ring[:, 2, :]).then_inc(S("sl_dn"), 1)

        @block.scalar
        def _(act):
            ld = lambda dst, src, sem="par_in": act.dma_start(dst, src).then_inc(S(sem), 16)
            ld(pst[0:KW, :], A["conf_dw_w"][0])
            for row, name in ((R_DWB, "conf_dw_b"), (R_LNG, "conf_ln_g"), (R_LNB, "conf_ln_b"), (R_NG, "ssm_norm_g")):
                ld(pst[row:row + 1, :], A[name])
            ld(sst[0:SW, :], A["ssm_conv_w"][0])
            ld(sst[SW:SW + 1, :], A["ssm_conv_b"])
            ld(sstate, A["state_ssm_conv"][0].rearrange("b t c -> (b t) c"))
            for h in range(2):
                ld(cstate[h], A["state_conf_conv"][0, 4 * h:4 * h + 4].rearrange("b t c -> (b t) c"))
            ld(lnmix[:, :], A["ln_mix"].rearrange("a (p k) -> (a p) k", k=KD))
            row = lambda name, n: A[name][0:1, :].to_broadcast([P, n])
            ld(dtb[:, :], row("ssm_dt_bias", H), "ssm_in")
            ld(alog[:, :], row("ssm_a_log", H), "ssm_in")
            for hh in range(2):
                ld(dsk[64 * hh:64 * hh + 64, :], A["ssm_d"][0:1, hh:H:2].to_broadcast([HD, NC]), "ssm_in")
            ld(lnffn[:, :], A["ln_ffn"].rearrange("a (p k) -> (a p) k", k=KD), "ssm_in")
            act.dma_start(O["new_conf_conv_sample"][0, :, 0:HIST - TB, :], A["state_conf_conv"][0, :, TB:HIST, :])\
                .then_inc(S("keep_out"), 16)

            act.wait_ge(S("x_in"), 48)
            act.wait_ge(S("eps"), 1)
            for r, (t0, n) in enumerate(TILES):
                act.activation(yf[0:n, D:2 * D], xt[0:n, r, :], ACT.Square, accum_out=ssq[0:n, r:r + 1])\
                    .then_inc(S("sq"), 1)
                act.wait_ge(S("sq"), r + 1)
            act.activation(rst[:, 0:3], ssq[:, 0:3], ACT.Sqrt, scale=1.0 / D, bias=ssq[:, 7:8]).then_inc(S("rt"), 1)

            pt = got(act, "par")
            act.activation(par[:, :, :].rearrange("p c r -> p (c r)"), pt[:, 0:NC * N_PAR], ACT.Copy)\
                .then_inc(free["act"], 1)
            pt = got(act, "spar")
            act.activation(spar[:, :, :].rearrange("p c r -> p (c r)"), pt[:, 0:60], ACT.Copy)
            act.wait_ge(S("consts"), 1)
            for c in range(XC_N):
                ins = act.activation(xb_seq[:, c, :, 0:SH],
                                     pt[:, 60 + 24 * c:84 + 24 * c].rearrange("p (b t) -> p b t", b=NB), ACT.Copy)
            ins.then_inc(free["act"], 1)
            for h in range(2):
                for q in range(2):
                    pt = got(act, "cst", h, q)
                    for c in range(4):
                        ins = act.activation(u_seq[:, 4 * q + c, 4 * h:4 * h + 4, 0:HIST],
                                             pt[:, 120 * c:120 * c + 120].rearrange("p (b t) -> p b t", b=4), ACT.Copy)
                    ins.then_inc(free["act"], 1)

            act.dma_start(wdt, w_in[:, :, C_DT:C_DT + H]).then_inc(S("wdt_in"), 16)
            for c in range(NC):
                b = c % 2
                pt = got(act, "in", "b", c)
                if c >= 2:
                    act.wait_ge(S("glu"), c - 1)
                act.activation(sig[b], pt[:, 0:T], ACT.Sigmoid).then_inc(free["act"], 1)
                pt = got(act, "in", "a", c)
                act.activation(uac[b], pt[:, 0:T], ACT.Copy).then_inc(free["act"], 1)
            pt = got(act, "in", "dt", 0)
            act.wait_ge(S("glu"), NC)
            act.activation(dtr, pt[0:H, 0:T], ACT.Copy).then_inc(free["act"], 1)

            def rows_out(dst, pt, q):
                act.activation(dst[:, 512 * q:512 * q + 512], pt[0:dst.shape[0], :], ACT.Copy)\
                    .then_inc(free["act"], 1)

            for c in range(XC_N):
                pt = got(act, "in", "x", c)
                act.activation(xb[:, c, SH:SH + TP], pt[:, 0:TP], ACT.Copy)
                act.activation(xs[:, c, :], pt[:, TP:T], ACT.Copy).then_inc(free["act"], 1)
                if c == 0:
                    pt = got(act, "dtT")
                    for r in range(3):
                        n = TILES[r][1]
                        ins = act.activation(dtk[0:n, r, :], pt[0:n, H * r:H * r + H], ACT.Copy)
                    ins.then_inc(free["act"], 1)
                if c == 1:
                    for q in range(2):
                        rows_out(ut_rows, got(act, "ut", q), q)
                    for q in range(2):
                        rows_out(us_rows, got(act, "us", q), q)
                    after_read(act, "us", 1)
                    act.dma_start(O["new_conf_conv_prompt"][0, 0], ut_rows).then_inc(S("u_out"), 16)
                    for b in range(NB):
                        act.dma_start(O["new_conf_conv_sample"][0, b, HIST - TB:HIST, :],
                                      us_rows[TB * b:TB * b + TB, :]).then_inc(S("u_out"), 16)
            for c in range(NC):
                pt = got(act, "in", "z", c)
                act.activation(zz[:, c, :], pt[:, 0:T], ACT.Silu).then_inc(free["act"], 1)
                if c == 1:
                    for q in range(3):
                        rows_out(xtail_rows, got(act, "xtail", q), q)
                    for q in range(3):
                        rows_out(xs_rows, got(act, "xs", q), q)
                    after_read(act, "xs", 2)
                    act.dma_start(O["new_ssm_conv_prompt"][0, 0], xtail_rows).then_inc(S("x_out"), 16)
                    for t in range(SH):
                        act.dma_start(O["new_ssm_conv_sample"][0, :, t, :], xs_rows[TB - SH + t:TS:TB, :])\
                            .then_inc(S("x_out"), 16)

            act.wait_ge(S("xconv"), XC_N)
            act.wait_ge(S("xconv_s"), 1)
            for q in range(3):
                v = xc[:, 4 * q:4 * q + 4, :]
                ins = act.activation(v, v, ACT.Silu)
            ins.then_inc(S("xact"), 1)
            act.activation(alog[:, :], alog[:, :], ACT.Exp)
            act.wait_ge(S("dt_abs"), 1)
            act.activation(sp[:, 1, :], sp[:, 0, :], ACT.Exp, scale=-1.0).then_inc(S("dt_exp"), 1)
            act.wait_ge(S("v_mean"), 1)
            act.wait_ge(S("x_out"), 16 * (1 + SH))
            act.activation(yt[:, :, :], vv[:, :, :], ACT.Square).then_inc(S("vsq"), 1)
            pt = got(act, "var")
            act.activation(yt[:, 0, :], pt[:, 0:T], ACT.Sqrt, scale=1.0 / D, bias=ssq[:, 7:8]).then_inc(free["act"], 1)
            act.wait_ge(S("v_norm"), 1)
            for c in range(NC):
                ins = act.activation(vv[:, c, :], vv[:, c, :], ACT.Silu, scale=par[:, c, R_LNG:R_LNG + 1],
                                     bias=par[:, c, R_LNB:R_LNB + 1])
            ins.then_inc(S("v_done"), 1)
            for r, (t0, n) in enumerate(TILES):
                after_read(act, "acum", r)
                if r > 0:
                    act.wait_ge(S("xw"), r)
                act.activation(dte[0:n, :], na[0:n, H:2 * H], ACT.Exp, scale=-1.0).then_inc(S("dte"), 1)
                v = seg if r < 2 else segs
                for q in range(4):
                    after_read(act, "seg", r, q)
                    act.activation(v[0:n, 4 * q:4 * q + 4, :], v[0:n, 4 * q:4 * q + 4, :], ACT.Exp)\
                        .then_inc(S("segexp"), 1)
                if r == 1:
                    for q in range(2):
                        pt = got(act, "eb", r, q)
                        act.activation(eb[:, 4 * q:4 * q + 4, :], pt[:, :].rearrange("p (c i) -> p c i", c=4), ACT.Exp)\
                            .then_inc(free["act"], 1)
                    for q in range(2):
                        pt = got(act, "hpT", q)
                        act.activation(hpt[:, 4 * q:4 * q + 4, :], pt[:, :].rearrange("p (c i) -> p c i", c=4),
                                       ACT.Copy).then_inc(free["act"], 1)
                if r == 2:
                    act.wait_ge(S("hp_done"), 1)
                    pt = got(act, "eb", r, 0)
                    act.activation(ebs, pt[:, :].rearrange("p (c i) -> p c i", c=NC), ACT.Exp)\
                        .then_inc(free["act"], 1)
            act.wait_ge(S("hp_out"), 16)
            for c in range(NC):
                if c >= 2:
                    act.wait_ge(filled, J[("yos", c - 2)] + 1)
                for q in range(2):
                    pt = got(act, "h0T", c, q)
                    act.activation(h0t[c % 2][:, 4 * q:4 * q + 4, :], pt[:, :].rearrange("p (b n) -> p b n", b=4),
                                   ACT.Copy).then_inc(free["act"], 1)
            act.wait_ge(S("gated"), 1)
            act.activation(sq, yt[:, :, :], ACT.Square).then_inc(S("ysq"), 1)
            for g, name in enumerate(("rms", "rms1")):
                pt = got(act, name)
                act.activation(rs[:, g, :], pt[:, 0:T], ACT.Sqrt, scale=1.0 / (D // G), bias=ssq[:, 7:8])\
                    .then_inc(free["act"], 1)

            def rms_rows(sem_in, sem_sq, sem_rt):
                for r, (t0, n) in enumerate(TILES):
                    act.wait_ge(sem_in, r + 1)
                    act.activation(yf[0:n, D:2 * D], xt[0:n, r, :], ACT.Square, accum_out=ssq[0:n, r:r + 1])\
                        .then_inc(sem_sq, 1)
                    act.wait_ge(sem_sq, r + 1)
                act.activation(rst[:, 0:3], ssq[:, 0:3], ACT.Sqrt, scale=1.0 / D, bias=ssq[:, 7:8]).then_inc(sem_rt, 1)

            rms_rows(S("x2"), S("sq2"), S("rt2"))
            act.dma_start(gfin, A["ln_final"].rearrange("(a d) -> a d", a=1).to_broadcast([P, D])).then_inc(S("gfin_in"), 16)
            for r, (t0, n) in enumerate(TILES):
                act.wait_ge(S("hn"), r + 1)
                act.dma_start(hn_dram[t0:t0 + n, :], hn[0:n, r, :]).then_inc(S("hn_out"), 16)
            act.wait_ge(S("g_in"), 1)
            act.activation(sg4[:, :, :], sg4[:, :, :], ACT.Exp).then_inc(S("g_exp"), 1)
            act.wait_ge(S("e_in"), 1)
            act.activation(cols[:, M_E, :], cols[:, M_T, :], ACT.Exp).then_inc(S("e_exp"), 1)

            def expert(i, b):
                e = 2 * i + b
                act.wait_ge(S("gu_done"), e + 1)
                wait(act, S("hid"), e - 1)
                act.activation(sil[b], bank[b][0:CAP, :], ACT.Silu).then_inc(S("sil"), 1)
                act.wait_ge(S("hid_T"), e + 1)
                wait(act, S("dn_done"), e - 1)
                act.activation(hidt[b], bank[4 + b][:, 0:4 * CAP].rearrange("p (k s) -> p k s", k=4), ACT.Copy)\
                    .then_inc(S("hidt"), 1)

            for b in range(2):
                expert(0, b)
            with act.Fori(1, NE // 2) as i:
                for b in range(2):
                    expert(i, b)
            over = act.value_load(mcount[0:1, 0:1], min_val=0, max_val=T)
            with act.If(over > CAP):
                with act.Fori(0, MAXPASS - 1) as q:
                    with act.Fori(0, NE) as e:
                        n = q * NE + e
                        act.wait_ge(S("sl_gu"), n + 1)
                        act.activation(sil[0], bank[0][0:CAP, :], ACT.Silu).then_inc(S("sl_sil"), 1)
                        act.wait_ge(S("sl_hT"), n + 1)
                        act.activation(hidt[0], bank[4][:, 0:4 * CAP].rearrange("p (k s) -> p k s", k=4), ACT.Copy)\
                            .then_inc(S("sl_hidt"), 1)
            rms_rows(S("x3"), S("sq3"), S("rt3"))
            act.wait_ge(S("keep_out"), 16)
            act.wait_ge(S("u_out"), 16 * (1 + NB))

        @block.vector
        def _(dve):
            own = [0]

            def link(ins):
                own[0] += 1
                ins.then_inc(S("dve_own"), 1)
                dve.wait_ge(S("dve_own"), own[0])

            tt_ = lambda out, a, b, op: dve.tensor_tensor(out, a, b, op)
            stt = lambda out, a, s_, b, op0, op1: dve.scalar_tensor_tensor(out=out, in0=a, scalar=s_, in1=b,
                                                                           op0=op0, op1=op1)
            dve.wait_ge(S("rt"), 1)
            link(dve.reciprocal(rst[:, 3:6], rst[:, 0:3]))
            for r, (t0, n) in enumerate(TILES):
                dve.tensor_scalar(xt[0:n, r, :], xt[0:n, r, :], rst[0:n, 3 + r:4 + r], None, ALU.mult)\
                    .then_inc(S("xn"), 1)
            dve.wait_ge(S("par_in"), 16 * 11)
            for r, (t0, n) in enumerate(TILES):
                for q in range(2):
                    pt = got(dve, "xt", r, q)
                    v = pt[:, :].rearrange("p (k t) -> p k t", k=4)[:, :, 0:n]
                    tt_(ht[:, 4 * q:4 * q + 4, toks(r)], v,
                        bc(lnmix[:, 4 * q:4 * q + 4].unsqueeze(2), [P, 4, n]), ALU.mult).then_inc(free["dve"], 1)

            def conv(src, dst, w, bias_row, taps, chunks, ready, sem, step):
                n = 0
                for c0 in range(0, chunks, 2):
                    ready(c0 + 1)
                    for k in range(taps):
                        for c in (c0, c0 + 1):
                            v, o = src[:, c, k:k + TP], dst[:, c, 0:TP]
                            if k == 0:
                                ins = dve.tensor_scalar(o, v, w[:, c, 0:1], w[:, c, bias_row:bias_row + 1],
                                                        ALU.mult, ALU.add)
                            else:
                                dve.wait_ge(step, n if k == taps - 1 and c > c0 else n - 1)
                                ins = stt(o, v, w[:, c, k:k + 1], o, ALU.mult, ALU.add)
                            if k < taps - 1:
                                ins.then_inc(step, 1)
                                n += 1
                            else:
                                ins.then_inc(sem, 1)

            after_read(dve, "par")
            conv(u, vv, par, R_DWB, KW, NC, lambda c: dve.wait_ge(S("glu"), c + 1), S("conv"), S("tap"))
            after_read(dve, "dtT")
            dve.wait_ge(S("ssm_in"), 16 * 5)
            dve.wait_ge(S("consts"), 1)
            link(tt_(dtk[:, :, :], dtk[:, :, :], bc(dtb[:, :].unsqueeze(1), [P, 3, H]), ALU.add))
            d48 = dtk[:, :, :].rearrange("p r h -> p (r h)")
            stt(sp[:, 0, :], d48, -1.0, d48, ALU.mult, ALU.max).then_inc(S("dt_abs"), 1)
            dve.wait_ge(S("u_out"), 16 * (1 + NB))
            conv(xb, xc, spar, SW, SW, XC_N, lambda c: after_read(dve, "in", "x", c), S("xconv"), S("xtap"))

            dve.wait_ge(S("dt_exp"), 1)
            link(dve.tensor_scalar(sp[:, 2, :], sp[:, 1, :], 2.0, None, ALU.add))
            link(dve.reciprocal(sp[:, 2, :], sp[:, 2, :]))
            link(tt_(sp[:, 1, :], sp[:, 1, :], sp[:, 2, :], ALU.mult))
            link(tt_(sp[:, 2, :], sp[:, 1, :], sp[:, 1, :], ALU.mult))
            link(dve.tensor_scalar(sp[:, 3, :], sp[:, 2, :], 1.0 / 17, None, ALU.mult))
            for k in (15, 13, 11, 9, 7, 5, 3):
                link(stt(sp[:, 3, :], sp[:, 3, :], 1.0 / k, sp[:, 2, :], ALU.add, ALU.mult))
            link(stt(sp[:, 3, :], sp[:, 3, :], 1.0, sp[:, 1, :], ALU.add, ALU.mult))
            link(dve.tensor_scalar(sp[:, 4, :], d48, 0.0, None, ALU.max))
            link(stt(d48, sp[:, 3, :], 2.0, sp[:, 4, :], ALU.mult, ALU.add))
            stt(dta[:, :, :], dtk[:, :, :], -1.0, bc(alog[:, :].unsqueeze(1), [P, 3, H]), ALU.mult, ALU.mult)\
                .then_inc(S("dta"), 1)

            pt = got(dve, "mean")
            stt(vv[:, :, :], bc(pt[:, 0:T].unsqueeze(1), [P, NC, T]), -1.0 / D, vv[:, :, :], ALU.mult, ALU.add)\
                .then_inc(free["dve"], 1)
            after_read(dve, "mean")
            dve.sem_inc(S("v_mean"), 1)
            after_read(dve, "var")
            link(dve.reciprocal(yt[:, 0, :], yt[:, 0, :]))
            tt_(vv[:, :, :], vv[:, :, :], bc(yt[:, 0:1, :], [P, NC, T]), ALU.mult).then_inc(S("v_norm"), 1)
            dve.wait_ge(S("v_norm"), 1)

            dve.wait_ge(S("x_out"), 16 * (1 + SH))
            for r, (t0, n) in enumerate(TILES):
                sg, m_tri = (seg, tri) if r < 2 else (segs, trib)
                for q in range(2):
                    pt = got(dve, "xT", r, q)
                    tt_(xdt[0:n, r, 512 * q:512 * q + 512].rearrange("p (h c) -> p h c", h=8),
                        pt[0:n, :].rearrange("p (h c) -> p h c", h=8),
                        bc(dtk[0:n, r, 8 * q:8 * q + 8].unsqueeze(2), [n, 8, HD]), ALU.mult).then_inc(free["dve"], 1)
                pt = got(dve, "bT", r)
                dve.tensor_copy(bt[0:n, r, :], pt[0:n, 0:G * NS]).then_inc(free["dve"], 1)
                pt = got(dve, "acum", r)
                dve.tensor_scalar(na[0:n, :], pt[0:n, 0:2 * H], -1.0, None, ALU.mult).then_inc(free["dve"], 1)
                pt = got(dve, "cb", r)
                tt_(cbm[0:n, :, 0:n], pt[0:n, 0:2 * P].rearrange("p (g i) -> p g i", g=G)[:, :, 0:n],
                    bc(m_tri[0:n, 0:n].unsqueeze(1), [n, G, n]), ALU.mult).then_inc(free["dve"], 1)
                after_read(dve, "cb", r)
                for q in range(4):
                    pt = got(dve, "seg", r, q)
                    for k in range(4):
                        hd = 4 * q + k
                        ins = dve.tensor_scalar(sg[0:n, hd, :], pt[0:n, n * k:n * k + n], na[0:n, hd:hd + 1], 0.0,
                                                ALU.add, ALU.min)
                    ins.then_inc(free["dve"], 1)
                dve.wait_ge(S("dte"), r + 1)
                if r > 0:
                    dve.wait_ge(filled, J[("st", r - 1, 1)] + 1)
                tt_(xw[0:n, :].rearrange("p (h c) -> p h c", h=H), xdt[0:n, r, :].rearrange("p (h c) -> p h c", h=H),
                    bc(dte[0:n, :].unsqueeze(2), [n, H, HD]), ALU.mult).then_inc(S("xw"), 1)
                for q in range(4):
                    dve.wait_ge(S("segexp"), 4 * r + q + 1)
                    ins = tt_(sg[0:n, 4 * q:4 * q + 4, :], sg[0:n, 4 * q:4 * q + 4, :],
                              bc(cbm[0:n, q // 2:q // 2 + 1, 0:n], [n, 4, n]), ALU.mult)
                ins.then_inc(S("mdone"), 1)
                c4 = lambda t: t[:, :].rearrange("p (c i) -> p c i", c=4)
                if r == 1:
                    after_read(dve, "eb", 1, 1)
                    for q in range(2):
                        pt = got(dve, "yo", q)
                        tt_(yt[:, 4 * q:4 * q + 4, toks(r)], c4(pt), eb[:, 4 * q:4 * q + 4, :], ALU.mult)\
                            .then_inc(free["dve"], 1)
                    after_read(dve, "yo", 1)
                if r < 2:
                    for q in range(2):
                        pt = got(dve, "yd", r, q)
                        v = yt[:, 4 * q:4 * q + 4, toks(r)]
                        ins = dve.tensor_copy(v, c4(pt)) if r == 0 else tt_(v, v, c4(pt), ALU.add)
                        ins.then_inc(free["dve"], 1)
                    for q in range(2):
                        pt = got(dve, "st", r, q)
                        if r == 0:
                            ins = dve.tensor_copy(hp[:, 4 * q:4 * q + 4, :], c4(pt))
                        else:
                            for k in range(4):
                                c = 4 * q + k
                                ins = stt(hp[:, c, :], hp[:, c, :], eb[:, c, P - 1:P], pt[:, P * k:P * k + P],
                                          ALU.mult, ALU.add)
                        ins.then_inc(free["dve"], 1)
                    if r == 1:
                        after_read(dve, "st", 1, 1)
                        dve.sem_inc(S("hp_done"), 1)
            dve.wait_ge(filled, J[("yd", 1, 1)] + 1)
            tt_(bm, bc(bt[0:TS, 2:3, :], [TS, 4, G * NS]), bc(bmask[:, :].unsqueeze(2), [TS, 4, G * NS]), ALU.mult)\
                .then_inc(S("bm"), 1)
            pt = got(dve, "yds")
            dve.tensor_copy(yt[:, :, TP:T], pt[:, :].rearrange("p (c i) -> p c i", c=NC)).then_inc(free["dve"], 1)
            after_read(dve, "yds")
            after_read(dve, "eb", 2, 0)
            for c in range(NC):
                for q in range(2):
                    pt = got(dve, "sts", c, q)
                    for k in range(4):
                        b = 4 * q + k
                        v = h0[c % 4][:, b, :]
                        ins = stt(v, v, ebs[:, c, TB * b + TB - 1:TB * b + TB], pt[:, P * k:P * k + P],
                                  ALU.mult, ALU.add)
                    ins.then_inc(free["dve"], 1)
                after_read(dve, "sts", c, 1)
                dve.sem_inc(S("h0_new"), 1)
                pt = got(dve, "yos", c)
                if c >= 1:
                    dve.wait_ge(S("dve_own"), own[0])
                tt_(ebs[:, c, :], ebs[:, c, :], pt[:, 0:TS], ALU.mult).then_inc(free["dve"], 1)
                after_read(dve, "yos", c)
                tt_(yt[:, c, TP:T], yt[:, c, TP:T], ebs[:, c, :], ALU.add)
            link(dve.tensor_copy(rst[:, 6:7], rst[:, 0:1]))
            for c in range(NC):
                ins = stt(yt[:, c, :], xc[:, c, :], dsk[:, c:c + 1], yt[:, c, :], ALU.mult, ALU.add)
            link(ins)
            tt_(yt[:, :, :], yt[:, :, :], zz[:, :, :], ALU.mult).then_inc(S("gated"), 1)
            for g, name in enumerate(("rms", "rms1")):
                after_read(dve, name)
                link(dve.reciprocal(rs[:, g, :], rs[:, g, :]))
                for k in range(4):
                    c = 4 * g + k
                    ins = stt(yt[:, c, :], yt[:, c, :], par[:, c, R_NG:R_NG + 1], rs[:, g, :], ALU.mult, ALU.mult)
            ins.then_inc(S("y_done"), 1)

            dve.wait_ge(S("x_again"), 48)
            for r in range(2):
                for q in range(2):
                    pt = got(dve, "out", r, q)
                    v = xt[:, r, 512 * q:512 * q + 512]
                    tt_(v, v, pt[:, :], ALU.add).then_inc(free["dve"], 1)
                after_read(dve, "out", r, 1)
                dve.sem_inc(S("x2"), 1)
            pt = got(dve, "outs")
            for q in range(2):
                v = xt[0:TS, 2, 512 * q:512 * q + 512]
                ins = tt_(v, v, pt[64 * q:64 * q + 64, :], ALU.add)
            ins.then_inc(free["dve"], 1)
            after_read(dve, "outs")
            dve.sem_inc(S("x2"), 1)
            dve.wait_ge(S("rt2"), 1)
            link(dve.reciprocal(rst[:, 3:6], rst[:, 0:3]))
            for r, (t0, n) in enumerate(TILES):
                dve.tensor_scalar(hn[0:n, r, :], xt[0:n, r, :], rst[0:n, 3 + r:4 + r], None, ALU.mult)\
                    .then_inc(S("hn"), 1)
            for r, (t0, n) in enumerate(TILES):
                for q in range(2):
                    pt = got(dve, "h2", r, q)
                    v = pt[:, :].rearrange("p (k t) -> p k t", k=4)[:, :, 0:n]
                    tt_(h2t[:, 4 * q:4 * q + 4, toks(r)], v,
                        bc(lnffn[:, 4 * q:4 * q + 4].unsqueeze(2), [P, 4, n]), ALU.mult).then_inc(free["dve"], 1)

            link(dve.memset(lg[:, :, :], 0.0))
            dve.wait_ge(S("rconst"), 1)
            pt = got(dve, "lg")
            tt_(lg[:, 0:2, :], pt[:, 0:72].rearrange("p (r n) -> p r n", r=2), bc(rbias.unsqueeze(1), [P, 2, 36]), ALU.add)
            tt_(lg[0:TS, 2, :], pt[0:TS, 72:108], rbias[0:TS, :], ALU.add).then_inc(free["dve"], 1)
            after_read(dve, "lg")

            def col(n):
                return cols[:, n, :]

            def wide(n, w):
                return bc(cols[:, n, :].unsqueeze(2), [P, 3, w])

            def first_max(vals, w, mx, out, desc, tmp_):
                link(dve.tensor_reduce(col(mx), vals, AX.X, ALU.max))
                link(tt_(tmp_, vals, wide(mx, w), ALU.is_equal))
                link(tt_(tmp_, tmp_, bc(desc.unsqueeze(1), [P, 3, w]), ALU.mult))
                link(dve.tensor_reduce(col(M_T), tmp_, AX.X, ALU.max))
                link(tt_(out, tmp_, wide(M_T, w), ALU.is_equal))

            groups = lg[:, :, 0:NG]
            first_max(groups, NG, M_SSUM, og, desc4, t4)
            tt_(sg4, groups, wide(M_SSUM, NG), ALU.subtract).then_inc(S("g_in"), 1)
            by_expert = lambda t: t.rearrange("p r (g e) -> p r g e", g=NG)
            for g in range(NG):
                o = le if g == 0 else t8
                link(tt_(o, lg[:, :, NG + EG * g:NG + EG * g + EG], bc(og[:, :, g:g + 1], [P, 3, EG]), ALU.mult))
                if g:
                    link(tt_(le, le, t8, ALU.add))
            first_max(le, EG, M_M1, o1, desc8, s8)
            link(stt(le, o1, -3.0e38, le, ALU.mult, ALU.add))
            first_max(le, EG, M_M2, o2, desc8, s8)
            tt_(col(M_T), col(M_M2), col(M_M1), ALU.subtract).then_inc(S("e_in"), 1)
            dve.wait_ge(S("g_exp"), 1)
            link(dve.tensor_reduce(col(M_G1), sg4, AX.X, ALU.add))
            link(dve.reciprocal(col(M_G1), col(M_G1)))
            dve.wait_ge(S("e_exp"), 1)
            link(dve.tensor_scalar(col(M_R), col(M_E), 1.0, None, ALU.add))
            link(dve.reciprocal(col(M_R), col(M_R)))
            link(tt_(col(M_W1), col(M_G1), col(M_R), ALU.mult))
            link(tt_(col(M_W2), col(M_W1), col(M_E), ALU.mult))
            for g in range(NG):
                for ee, oo in ((e1, o1), (e2, o2)):
                    tt_(ee[:, :, EG * g:EG * g + EG], oo, bc(og[:, :, g:g + 1], [P, 3, EG]), ALU.mult)
            link(dve.tensor_copy(t8, o1))
            for ee in (e1, e2):
                link(dve.memset(ee[TS:P, 2, :], 0.0))
            tt_(aa, e1, e2, ALU.add).then_inc(S("chosen"), 1)
            pt = got(dve, "rank")
            dve.tensor_copy(pos, pt[:, 0:3 * NE].rearrange("p (r n) -> p r n", r=3))
            dve.tensor_copy(cnt, pt[:, 3 * NE:4 * NE]).then_inc(free["dve"], 1)
            after_read(dve, "rank")
            link(dve.tensor_reduce(cols[:, M_T, 0:1], cnt, AX.X, ALU.max))
            dve.tensor_copy(mcount, cols[:, M_T, 0:1]).then_inc(S("count_ready"), 1)
            dve.wait_ge(S("count_ready"), 1)
            for ee, m in ((e1, M_S1), (e2, M_S2)):
                link(tt_(t32, ee, pos, ALU.mult))
                link(dve.tensor_reduce(col(m), t32, AX.X, ALU.add))
            for w, (ee, mw) in enumerate(((e1, M_W1), (e2, M_W2))):
                link(dve.tensor_scalar(col(M_T), tokid.unsqueeze(1)[:, 0, :], -BIG, None, ALU.add))
                tt_(val[w][:, :, 0, :], ee, wide(M_T, NE), ALU.mult)
                link(dve.tensor_scalar(col(M_E), tokid, 2.0, float(w) - BIG, ALU.mult, ALU.add))
                tt_(val[w][:, :, 1, :], ee, wide(M_E, NE), ALU.mult)
                link(tt_(val[w][:, :, 2, :], ee, wide(mw, NE), ALU.mult))

            def slot_select():
                for r in range(3):
                    for w, m in enumerate((M_S1, M_S2)):
                        ins = dve.tensor_scalar(osel[:, r, w, :], slotno, cols[:, m, r:r + 1], None, ALU.is_equal)
                return ins

            def slot_indices(pt):
                dve.tensor_scalar(gidx[:, 0:NE], pt[:, 0:NE], BIG, None, ALU.add)
                dve.tensor_scalar(sidx[:, 0:NE], pt[:, NE:2 * NE], 2.0, halfrow, ALU.mult, ALU.add)
                return dve.tensor_copy(wsl[:, 0:NE], pt[:, 2 * NE:3 * NE])

            slot_select().then_inc(S("osel"), 1)
            slot_indices(got(dve, "slots")).then_inc(free["dve"], 1)
            after_read(dve, "slots")
            dve.sem_inc(S("idx"), 1)

            def tokens(b):
                return tt_(xgt[b], bank[2 + b][:, :].rearrange("p (k s) -> p k s", k=KD),
                           bc(lnffn[:, :].unsqueeze(2), [P, KD, CAP]), ALU.mult)

            dve.wait_ge(S("xg_T"), 1)
            tokens(0).then_inc(S("xgt"), 1)

            def expert(i, b):
                e = 2 * i + b
                dve.wait_ge(S("sil"), e + 1)
                wait(dve, S("hid_T"), e - 1)
                tt_(hid[b], sil[b], bank[b][CAP:P, :], ALU.mult).then_inc(S("hid"), 1)
                dve.wait_ge(S("xg_T"), e + 2)
                wait(dve, S("gu_done"), e)
                tokens(1 - b).then_inc(S("xgt"), 1)
                dve.wait_ge(S("dn_done"), e + 1)
                wait(dve, S(f"scat{b}"), 16 * i)
                dve.tensor_scalar(yo[b], bank[6 + b][:, :], wsl[:, bass.ds(e, 1)], None, ALU.mult)\
                    .then_inc(S("yo"), 1)

            for b in range(2):
                expert(0, b)
            with dve.Fori(1, NE // 2) as i:
                for b in range(2):
                    expert(i, b)
            over = dve.value_load(mcount[0:1, 0:1], min_val=0, max_val=T)
            with dve.If(over > CAP):
                dve.wait_ge(S("scat0"), 16 * NE // 2)
                with dve.Fori(0, MAXPASS - 1) as q:
                    dve.wait_ge(S("sl_next"), q * NE + 1)
                    for m in (M_S1, M_S2):
                        ins = dve.tensor_scalar(col(m), col(m), -float(CAP), None, ALU.add)
                    ins.then_inc(S("sl_own"), 1)
                    dve.wait_ge(S("sl_own"), q + 1)
                    slot_select().then_inc(S("sl_osel"), 1)
                    dve.wait_ge(S("sl_slots"), q + 1)
                    slot_indices(bank[0]).then_inc(S("sl_idx"), 1)
                    wait_apart(dve, S("sl_idx"), q + 1)
                    with dve.Fori(0, NE) as e:
                        n = q * NE + e
                        dve.wait_ge(S("sl_xT"), n + 1)
                        tokens(0).then_inc(S("sl_x"), 1)
                        dve.wait_ge(S("sl_sil"), n + 1)
                        tt_(hid[0], sil[0], bank[0][CAP:P, :], ALU.mult).then_inc(S("sl_hid"), 1)
                        dve.wait_ge(S("sl_dn"), n + 1)
                        dve.tensor_scalar(yo[0], bank[6][:, :], wsl[:, bass.ds(e, 1)], None, ALU.mult)\
                            .then_inc(S("sl_y"), 1)

            dve.wait_ge(S("ye_in"), 48)
            for r, (t0, n) in enumerate(TILES):
                link(tt_(xt[0:n, r, :], xt[0:n, r, :], ring[0:n, r, 0:D], ALU.add))
                tt_(xt[0:n, r, :], xt[0:n, r, :], ring[0:n, r, D:2 * D], ALU.add).then_inc(S("x3"), 1)
            dve.wait_ge(S("rt3"), 1)
            link(dve.reciprocal(rst[:, 3:6], rst[:, 0:3]))
            dve.wait_ge(S("gfin_in"), 16)
            for r, (t0, n) in enumerate(TILES):
                stt(xt[0:n, r, :], xt[0:n, r, :], rst[0:n, 3 + r:4 + r], gfin[0:n, :], ALU.mult, ALU.mult)\
                    .then_inc(S("y_final"), 1)


_INS = ["x_prompt", "x_sample", "state_conf_conv", "state_ssm_conv", "state_ssm", "ln_mix", "w_in", "conf_dw_w",
        "conf_dw_b", "conf_ln_g", "conf_ln_b", "ssm_conv_w", "ssm_conv_b", "ssm_dt_bias", "ssm_a_log", "ssm_d",
        "ssm_norm_g", "w_out", "ln_ffn", "router_group_w", "router_group_b", "router_expert_w", "router_expert_b",
        "expert_w_gate", "expert_w_up", "expert_w_down", "ln_final"]
_OUTS = [("y_prompt", (1, TP, D)), ("y_sample", (NB, TB, D)), ("new_conf_conv_prompt", (1, 1, HIST, D)),
         ("new_ssm_conv_prompt", (1, 1, SH, XBC)), ("new_ssm_prompt", (1, 1, H, HD, NS)),
         ("new_conf_conv_sample", (1, NB, HIST, D)), ("new_ssm_conv_sample", (1, NB, SH, XBC)),
         ("new_ssm_sample", (1, NB, H, HD, NS))]


def kernel(**inputs):
    import numpy as _np
    import concourse.bacc as _bacc
    from concourse.bass_utils import run_bass_kernel_spmd as _run

    nc = _bacc.Bacc("TRN2", target_bir_lowering=False, num_devices=1)
    arrays, ins, outs = {}, {}, {}
    for name in _INS:
        a = _np.ascontiguousarray(inputs[name])
        arrays[f"in_{name}"] = a
        ins[name] = nc.dram_tensor(f"in_{name}", a.shape, mybir.dt.from_np(a.dtype), kind="ExternalInput").ap()
    for name, shape in _OUTS:
        outs[name] = nc.dram_tensor(f"out_{name}", shape, F32, kind="ExternalOutput").ap()
    build(nc, ins, outs)
    r = _run(nc, [arrays], core_ids=[0])
    return tuple(r.results[0][f"out_{name}"] for name, _ in _OUTS)
```

```python
from contextlib import ExitStack

import concourse.bass as bass
from concourse import mybir

ALU = mybir.AluOpType
ACT = mybir.ActivationFunctionType
AX = mybir.AxisListType
F32 = mybir.dt.float32
I32 = mybir.dt.int32

P = 128
D = 1024
KD = D // P
TP = 256
NB, TB = 8, 8
TS = NB * TB
T = TP + TS
TILES = [(0, 128), (128, 128), (256, 64)]
NC = D // P
KW = 31
HIST = KW - 1
SW = 4
SH = SW - 1
H, HD, NS, G = 16, 64, 128, 2
XBC = D + 2 * G * NS
XC_N = XBC // P
C_UA, C_UB, C_Z, C_X, C_DT = 0, D, 2 * D, 3 * D, 3 * D + XBC
SEQ_W = HIST + TB
U_W = HIST + TP + NB * SEQ_W
XSEQ_W = SH + TB
X_W = SH + TP + NB * XSEQ_W
EPS = 1e-6
NE, EG, NG = 32, 8, 4
FE = 512
CAP = 64
MAXPASS = T // CAP
NC_POOL = 6
BIG = 8192.0

R = 6
UNIT = 4096
UNITS = ["ub0", "ua0", "ub1", "ua1", "x0", "x1", "x2", "z0", "z1", "o0", "o1", "o2", "o3"]
N_MIX = len(UNITS)

R_DWB, R_LNG, R_LNB, R_NG, N_PAR = KW, KW + 1, KW + 2, KW + 3, KW + 4


def bank_jobs():
    jobs = [(("xt", r, q), "dve") for r in range(3) for q in range(2)]
    for c in range(NC):
        jobs += [(("in", "b", c), "act")]
        if c == 0:
            jobs += [(("par",), "act"), (("spar",), "act")]
            jobs += [(("cst", h, q), "act") for h in range(2) for q in range(2)]
        jobs += [(("in", "a", c), "act")]
    jobs += [(("in", "dt", 0), "act")]
    for c in range(XC_N):
        jobs += [(("in", "x", c), "act")]
        if c == 0:
            jobs += [(("dtT",), "act")]
        if c == 1:
            jobs += [(("ut", q), "act") for q in range(2)] + [(("us", q), "act") for q in range(2)]
    for c in range(NC):
        jobs += [(("in", "z", c), "act")]
        if c == 1:
            jobs += [(("xtail", q), "act") for q in range(3)] + [(("xs", q), "act") for q in range(3)]
    jobs += [(("mean",), "dve")]
    for r in range(3):
        jobs += [(("xT", r, q), "dve") for q in range(2)] + [(("bT", r), "dve")]
        jobs += [(("acum", r), "dve"), (("cb", r), "dve")]
        jobs += [(("seg", r, q), "dve") for q in range(4)]
        if r == 0:
            jobs += [(("var",), "act")]
        if r > 0:
            jobs += [(("eb", r, q), "act") for q in range(2 if r < 2 else 1)]
        if r == 1:
            jobs += [(("hpT", q), "act") for q in range(2)]
        if r == 1:
            jobs += [(("yo", q), "dve") for q in range(2)]
        if r < 2:
            jobs += [((kind, r, q), "act" if r == 0 else "dve") for kind in ("yd", "st") for q in range(2)]
    jobs += [(("yds",), "dve")]
    jobs += [(("h0T", 0, q), "act") for q in range(2)]
    for c in range(NC):
        if c + 1 < NC:
            jobs += [(("h0T", c + 1, q), "act") for q in range(2)]
        jobs += [(("sts", c, q), "dve") for q in range(2)]
        jobs += [(("yos", c), "dve")]
    jobs += [(("rms",), "act")]
    jobs += [(("rms1",), "act")]
    jobs += [(("out", r, q), "dve") for r in range(2) for q in range(2)] + [(("outs",), "dve")]
    jobs += [(("h2", r, q), "dve") for r in range(3) for q in range(2)]
    jobs += [(("lg",), "dve"), (("rank",), "dve"), (("slots",), "dve")]
    return jobs


JOBS = bank_jobs()
J = {name: n for n, (name, _) in enumerate(JOBS)}
RANK = {}
for _who in ("act", "dve"):
    for _i, _n in enumerate([n for n, (_, who) in enumerate(JOBS) if who == _who]):
        RANK[_n] = _i


def build(nc, A, O):
    hn_dram = nc.dram_tensor("hn_scratch", (T, D), F32).ap()
    ye_dram = nc.dram_tensor("ye_scratch", (T * 4, D // 2), F32).ap()
    with ExitStack() as ctx:
        def sb(name, shape, dt=F32):
            return ctx.enter_context(nc.sbuf_tensor(name, shape, dt))

        sems = {}

        def S(name):
            if name not in sems:
                sems[name] = ctx.enter_context(nc.semaphore("s_" + name))
            return sems[name]

        bank = [ctx.enter_context(nc.psum_tensor(f"bank{i}", [P, 512], F32)) for i in range(8)]
        ring = sb("ring", [P, R, UNIT])
        xt = sb("xt", [P, 3, D])
        xtf = xt[:, :, :].rearrange("p r d -> p (r d)")
        ra = sb("region_a", [P, NC * U_W + KD * T])
        rb = sb("region_b", [P, XC_N * X_W])
        zz = sb("zz", [P, NC, T])
        vv = sb("vv", [P, NC, T])
        xc = sb("xc", [P, XC_N, T])
        yt = sb("yt", [P, NC, T])
        flat = lambda t: t[:, :, :].rearrange("p c t -> p (c t)")
        zf, vf, xcf, yf = flat(zz), flat(vv), flat(xc), flat(yt)

        ident = sb("ident", [P, P])
        tri = sb("tri", [P, P])
        later = sb("later", [P, P])
        before = sb("before", [P, P])
        trib = sb("trib", [TS, TS])
        laterb = sb("laterb", [TS, TS])
        ones = sb("ones", [P, P])
        bmask = sb("bmask", [TS, NB])
        par = sb("par", [P, NC, N_PAR])
        spar = sb("spar", [P, XC_N, SW + 1])
        lnmix = sb("lnmix", [P, KD])
        lnffn = sb("lnffn", [P, KD])
        dtb = sb("dtb", [P, H])
        alog = sb("alog", [P, H])
        dsk = sb("dsk", [P, NC])
        xs = sb("xs", [P, XC_N, TS])
        ssq = sb("ssq", [P, 8])
        rst = sb("rst", [P, 8])
        dtk = sb("dtk", [P, 3, H])
        dta = sb("dta", [P, 3, H])
        sp = sb("sp", [P, 5, 3 * H])
        na = sb("na", [P, 2 * H])
        dte = sb("dte", [P, H])

        u = ra[:, 0:NC * U_W].rearrange("p (c t) -> p c t", c=NC)
        u_seq = u[:, :, HIST + TP:].rearrange("p c (b w) -> p c b w", b=NB)
        ht = ra[:, NC * U_W:].rearrange("p (k t) -> p k t", k=KD)
        xb = rb[:, :].rearrange("p (c t) -> p c t", c=XC_N)
        xb_seq = xb[:, :, SH + TP:].rearrange("p c (b w) -> p c b w", b=NB)
        pst, sst, sstate = yf[0:N_PAR, 0:D], zf[0:SW + 1, 0:XBC], vf[0:NB * SH, 0:XBC]
        cstate = [xcf[0:4 * HIST, D * h:D * h + D] for h in range(2)]
        sig = [yf[:, D + T * b:D + T * b + T] for b in range(2)]
        uac = [yf[:, D + 2 * T + T * b:D + 2 * T + T * b + T] for b in range(1)]
        usc = vv[:, :, TP:T]
        tmp = xtf[:, 0:XC_N * TS]
        xs_rows = xtf[0:TS, 768:768 + XBC]
        wdt = xtf[:, 2304:2304 + KD * H].rearrange("p (k h) -> p k h", k=KD)
        uac.append(xtf[:, 2432:2432 + T])
        ut_rows, us_rows = xcf[0:HIST, 0:D], xcf[0:TS, D:2 * D]
        xtail_rows = yf[0:SH, 0:XBC]
        dtr = yf[0:H, 1600:1600 + T]
        xdt = rb[:, 0:3 * D].rearrange("p (r c) -> p r c", r=3)
        bt = rb[:, 3 * D:3 * D + 3 * G * NS].rearrange("p (r c) -> p r c", r=3)
        seg = ra[:, 0:H * P].rearrange("p (h i) -> p h i", h=H)
        segs = ra[0:TS, 0:H * TS].rearrange("p (h i) -> p h i", h=H)
        bm = ra[0:TS, 5120:7168].rearrange("p (b c) -> p b c", b=NB)
        eb = ra[:, 2048:3072].rearrange("p (c i) -> p c i", c=NC)
        ebs = ra[:, 2048:2560].rearrange("p (c i) -> p c i", c=NC)
        hp = ra[:, 3072:4096].rearrange("p (c n) -> p c n", c=NC)
        hpt = ra[:, 4096:5120].rearrange("p (c n) -> p c n", c=NC)
        h0t = [hp, hpt]
        h0 = [ring[:, (N_MIX + c // 4) % R, D * (c % 4):D * (c % 4) + D].rearrange("p (b n) -> p b n", b=NB)
              for c in range(NC)]
        xw = xtf[:, 0:D]
        cbm = rb[:, 3840:3840 + G * P].rearrange("p (g i) -> p g i", g=G)
        rs = ra[:, 0:2 * T].rearrange("p (g t) -> p g t", g=G)
        sq = rb[:, 0:NC * T].rearrange("p (c t) -> p c t", c=NC)
        h2t = ra[:, 0:KD * T].rearrange("p (k t) -> p k t", k=KD)
        hn = xcf[:, 0:3 * D].rearrange("p (r d) -> p r d", r=3)
        gat = [t[0:CAP, D:2 * D] for t in (yf, vf)]
        last_gate = rb[:, 0:UNIT]
        xgt = [ra[:, 2560 + 512 * b:3072 + 512 * b].rearrange("p (k s) -> p k s", k=KD) for b in range(2)]
        hidt = [ra[:, 3584 + 256 * b:3840 + 256 * b].rearrange("p (k s) -> p k s", k=4) for b in range(2)]
        sil = [zf[0:CAP, 512 * b:512 * b + 512] for b in range(2)]
        hid = [zf[0:CAP, 1024 + 512 * b:1536 + 512 * b] for b in range(2)]
        yo = [yf[:, 512 * b:512 * b + 512] for b in range(2)]
        wr = zf[:, 2048:2048 + KD * 36].rearrange("p (k n) -> p k n", k=KD)
        rbias = zf[:, 2336:2372]
        gfin = vf[:, 0:D]
        at = [4096]

        def moe(n):
            at[0] += n
            assert at[0] <= NC * U_W + KD * T
            return ra[:, at[0] - n:at[0]]

        r3 = lambda t: t.rearrange("p (r n) -> p r n", r=3)
        lg = r3(moe(3 * 36))
        e1, e2, aa, pos = (r3(moe(3 * NE)) for _ in range(4))
        og, sg4, t4 = (r3(moe(3 * NG)) for _ in range(3))
        le, o1, o2, s8, t8 = (r3(moe(3 * EG)) for _ in range(5))
        t32 = r3(moe(3 * NE))
        cols = moe(3 * 16).rearrange("p (n r) -> p n r", r=3)
        val = [moe(3 * 3 * NE).rearrange("p (r c e) -> p r c e", r=3, c=3) for _ in range(2)]
        osel = moe(3 * 2 * P).rearrange("p (r w s) -> p r w s", r=3, w=2)
        slotno = moe(P)
        desc4, desc8, tokid, halfrow = moe(NG), moe(EG), moe(3), moe(1)
        cnt, wsl = moe(NE), moe(NE + 1)
        gidx = moe(NE + 2).bitcast(I32)
        sidx = moe(NE + 1).bitcast(I32)
        gcur = [moe(1).bitcast(I32) for _ in range(2)]
        scur = [moe(1).bitcast(I32) for _ in range(2)]
        mcount = moe(1).bitcast(I32)
        sel0 = r3(moe(3 * CAP))
        wait_word = moe(6)
        M_SSUM, M_G1, M_M1, M_M2, M_E, M_R, M_W1, M_W2, M_S1, M_S2, M_T = range(11)

        def toks(r):
            return slice(TILES[r][0], TILES[r][0] + TILES[r][1])

        def bc(ap, shape):
            return ap.to_broadcast(shape)

        def wait(eng, sem, value):
            if isinstance(value, int) and value <= 0:
                return
            eng.wait_ge(sem, value)

        def wait_apart(eng, sem, value):
            eng.wait_ge(S("ident"), 1)
            eng.wait_ge(sem, value)

        filled = S("filled")
        free = {"act": S("act_read"), "dve": S("dve_read")}

        def take(pe, *name):
            n = J[name]
            if n >= 8:
                pe.wait_ge(free[JOBS[n - 8][1]], RANK[n - 8] + 1)
            return bank[n % 8]

        def got(eng, *name):
            eng.wait_ge(filled, J[name] + 1)
            return bank[J[name] % 8]

        def read_of(name):
            n = J[name]
            return free[JOBS[n][1]], RANK[n] + 1

        def after_read(eng, *name):
            eng.wait_ge(*read_of(name))

        ring_in = [S(f"ring_in{s}") for s in range(R)]

        def landed(eng, unit):
            n = UNITS.index(unit)
            eng.wait_ge(ring_in[n % R], 16 * (n // R + 1))
            return ring[:, n % R, :]

        slot_pre = [len([n for n in range(N_MIX) if n % R == s]) for s in range(R)]
        u_slot = [(N_MIX + m) % R for m in range(R)]
        ctx.enter_context(nc.allow_non_contiguous_dma(reason="small parameters and state rows"))
        block = ctx.enter_context(nc.Block())
        w_in = A["w_in"][0].rearrange("(p k) c -> p k c", k=KD)
        w_out = A["w_out"][0].rearrange("(c p) n -> p c n", p=P)

        def expert_src(m, e):
            w = [A["expert_w_gate"], A["expert_w_up"], A["expert_w_down"]][m % 3]
            v = w[0, bass.ds(e, 1)].rearrange("e a b -> (e a) b")
            return v.rearrange("(p k) f -> p (k f)", p=P)

        @block.sync
        def _(sp_):
            def load_x(r, sem):
                t0, n = TILES[r]
                src = A["x_prompt"][0, t0:t0 + n, :] if r < 2 else A["x_sample"].rearrange("b t d -> (b t) d")
                sp_.dma_start(xt[0:n, r, :], src).then_inc(sem, 16)

            for r in range(3):
                load_x(r, S(f"x_in{r}"))
            sp_.dma_start(lnmix[:, :], A["ln_mix"].rearrange("a (p k) -> (a p) k", k=KD)).then_inc(S("mix_in"), 16)
            last = {"ub0": ("in", "a", 3), "ua0": ("in", "a", 3), "ub1": ("in", "a", 7), "ua1": ("in", "a", 7),
                    "x0": ("in", "x", 3), "x1": ("in", "x", 7), "x2": ("in", "x", 11),
                    "z0": ("in", "z", 3), "z1": ("in", "z", 7)}
            col = {"ub": C_UB, "ua": C_UA, "x": C_X, "z": C_Z}

            def slot_free(n):
                if n >= R:
                    old = UNITS[n - R]
                    if old == "o3":
                        sp_.wait_ge(filled, J[("outs",)] + 1)
                    elif old[0] == "o":
                        sp_.wait_ge(S("wo_used"), int(old[1]) + 1)
                    else:
                        sp_.wait_ge(filled, J[last[old]] + 1)

            for n, unit in enumerate(UNITS):
                slot_free(n)
                kind, i = unit[:-1], int(unit[-1])
                if kind == "o":
                    dst, src = ring[:, n % R, :].rearrange("p (c n) -> p c n", c=4), w_out[:, 4 * i:4 * i + 4, :]
                else:
                    c0 = col[kind] + 512 * i
                    dst, src = ring[:, n % R, :].rearrange("p (k c) -> p k c", k=KD), w_in[:, :, c0:c0 + 512]
                sp_.dma_start(dst, src).then_inc(ring_in[n % R], 16)
                if n == 1:
                    ld = lambda dst, src: sp_.dma_start(dst, src).then_inc(S("par_in"), 16)
                    ld(pst[0:KW, :], A["conf_dw_w"][0])
                    for row, name in ((R_DWB, "conf_dw_b"), (R_LNG, "conf_ln_g"), (R_LNB, "conf_ln_b"),
                                      (R_NG, "ssm_norm_g")):
                        ld(pst[row:row + 1, :], A[name])
                    ld(sst[0:SW, :], A["ssm_conv_w"][0])
                    ld(sst[SW:SW + 1, :], A["ssm_conv_b"])
                    ld(sstate, A["state_ssm_conv"][0].rearrange("b t c -> (b t) c"))
                    for h in range(2):
                        ld(cstate[h], A["state_conf_conv"][0, 4 * h:4 * h + 4].rearrange("b t c -> (b t) c"))
            def first_expert_unit(m):
                slot_free(N_MIX + m)
                sp_.dma_start(ring[:, u_slot[m], :], expert_src(m, m // 3)).then_inc(ring_in[u_slot[m]], 16)

            pair = lambda t, c: t[0, :, 2 * c:2 * c + 2].rearrange("b h p n -> (h p) b n")

            for c in range(NC):
                if c % 4 == 0:
                    slot_free(N_MIX + c // 4)
                sp_.dma_start(h0[c], pair(A["state_ssm"], c)).then_inc(S(f"h0_in{c}"), 16)
            sp_.wait_ge(S("hp_done"), 1)
            sp_.dma_start(O["new_ssm_prompt"][0, 0].rearrange("(c h) p n -> (h p) c n", c=NC), hp)\
                .then_inc(S("hp_out"), 16)
            for c in range(NC):
                sp_.wait_ge(S("h0_new"), c + 1)
                sp_.dma_start(pair(O["new_ssm_sample"], c), h0[c]).then_inc(S(f"h0_out{c // 4}"), 16)
                if c == 5:
                    sp_.wait_ge(S("h0_out0"), 64)
                    first_expert_unit(0)
            sp_.wait_ge(filled, J[("sts", NC - 1, 1)] + 1)
            for r in range(3):
                load_x(r, S("x_again"))
            sp_.wait_ge(S("h0_out1"), 64)
            first_expert_unit(1)
            sp_.wait_ge(S("y_done"), 1)
            sp_.dma_start(last_gate, expert_src(0, NE - 1)).then_inc(S("last_gate_in"), 16)
            for m in range(2, R):
                first_expert_unit(m)

            def expert_unit(i, m):
                b = m // 3
                sp_.wait_ge(S("gu_done") if m % 3 < 2 else S("dn_done"), 2 * i + b - 1)
                sp_.dma_start(ring[:, u_slot[m], :], expert_src(m, 2 * i + b)).then_inc(ring_in[u_slot[m]], 16)

            with sp_.Fori(1, NE // 2 - 1) as i:
                for m in range(R):
                    expert_unit(i, m)
            for m in (0, 1, 2, 4, 5):
                expert_unit(NE // 2 - 1, m)
            sp_.wait_ge(S("count_ready"), 1)
            over = sp_.value_load(mcount[0:1, 0:1], min_val=0, max_val=T)
            with sp_.If(over > CAP):
                sp_.wait_ge(S("dn_done"), NE)
                with sp_.Fori(0, MAXPASS - 1) as q:
                    with sp_.Fori(0, NE) as e:
                        sp_.wait_ge(S("sl_next"), q * NE + e + 1)
                        for m in range(3):
                            sp_.dma_start(ring[:, m, :], expert_src(m, e)).then_inc(S("sl_w"), 16)
            sp_.wait_ge(S("ye_all"), 1)
            sp_.wait_ge(S("dn_done"), NE)
            ye_tok = ye_dram.rearrange("(t c) n -> t (c n)", c=4)
            for r, (t0, n) in enumerate(TILES):
                sp_.dma_start(ring[0:n, r, 0:2 * D], ye_tok[t0:t0 + n, :]).then_inc(S(f"ye_in{r}"), 16)
            for r, (t0, n) in enumerate(TILES):
                sp_.wait_ge(S("y_final"), r + 1)
                dst = O["y_prompt"][0, t0:t0 + n, :] if r < 2 else O["y_sample"].rearrange("b t d -> (b t) d")
                sp_.dma_start(dst, xt[0:n, r, :]).then_inc(S("y_out"), 16)
            sp_.wait_ge(S("y_out"), 48)
            sp_.wait_ge(S("hp_out"), 16)

        @block.gpsimd
        def _(pool):
            own = [0]

            def link(ins):
                own[0] += 1
                ins.then_inc(S("pool_own"), 1)
                pool.wait_ge(S("pool_own"), own[0])

            pool.memset(rst[:, :], 1.0)
            link(pool.memset(ssq[:, :], 0.0))
            pool.memset(ssq[:, 7:8], EPS).then_inc(S("eps"), 1)
            for m in (ident, before, later):
                pool.memset(m[:, :], 0.0)
            for m in (tri, ones, trib, laterb, bmask):
                pool.memset(m[:, :], 1.0)
            pool.memset(u[:, :, 0:HIST], 0.0)
            link(pool.memset(xb[:, :, 0:SH], 0.0))
            sel = lambda o, pat, op, fill, base, cm: pool.affine_select(
                out=o, in_=o, compare_op=op, fill=fill, base=base, pattern=pat, channel_multiplier=cm)
            sel(ident[:, :], [[-1, P]], ALU.not_equal, 1.0, 0, 1).then_inc(S("ident"), 1)
            sel(tri[:, :], [[1, P]], ALU.is_ge, 0.0, 0, -1)
            sel(later[:, :], [[1, P]], ALU.is_ge, 1.0, 0, -1)
            sel(before[:, :], [[-1, P]], ALU.is_ge, 1.0, 0, 1)
            sel(trib[:, :], [[1, TS]], ALU.is_ge, 0.0, 0, -1)
            link(sel(laterb[:, :], [[-1, TS]], ALU.is_gt, 0.0, 0, 1))
            for m in (trib, laterb):
                v = m[:, :].rearrange("p (b i) -> p b i", b=NB)
                link(sel(v, [[-TB, NB], [0, TB]], ALU.is_ge, 0.0, 0, 1))
                link(sel(v, [[TB, NB], [0, TB]], ALU.is_ge, 0.0, TB - 1, -1))
            link(sel(bmask[:, :], [[-TB, NB]], ALU.is_ge, 0.0, 0, 1))
            link(sel(bmask[:, :], [[TB, NB]], ALU.is_ge, 0.0, TB - 1, -1))
            pool.memset(dtk[:, :, :], 0.0).then_inc(S("consts"), 1)

            for c in range(NC):
                b = c % 2
                after_read(pool, "in", "a", c)
                pool.tensor_tensor(u[:, c, HIST:HIST + TP], uac[b][:, 0:TP], sig[b][:, 0:TP], ALU.mult)
                link(pool.tensor_tensor(usc[:, c, :], uac[b][:, TP:T], sig[b][:, TP:T], ALU.mult))
                pool.tensor_copy(u_seq[:, c, :, HIST:], usc[:, c, :].rearrange("p (b t) -> p b t", b=NB))\
                    .then_inc(S("glu"), 1)
            pool.wait_ge(S("glu"), NC)
            pool.wait_ge(*read_of(("cst", 1, 1)))
            w4 = lambda w, k, n: bc(w[:, 0:n, k:k + 1].unsqueeze(3), [P, n, NB, TB])
            acc = vv[:, 0:NC_POOL, TP:T].rearrange("p c (b t) -> p c b t", b=NB)
            tmp4 = tmp[:, 0:NC_POOL * TS].rearrange("p (c b t) -> p c b t", c=NC_POOL, b=NB)
            pool.wait_ge(filled, J[("us", 1)] + 1)
            link(pool.tensor_tensor(acc, u_seq[:, 0:NC_POOL, :, 0:TB], w4(par, 0, NC_POOL), ALU.mult))
            link(pool.tensor_tensor(acc, acc, w4(par, R_DWB, NC_POOL), ALU.add))
            for k in range(1, KW):
                link(pool.tensor_tensor(tmp4, u_seq[:, 0:NC_POOL, :, k:k + TB], w4(par, k, NC_POOL), ALU.mult))
                ins = pool.tensor_tensor(acc, acc, tmp4, ALU.add)
                if k < KW - 1:
                    link(ins)
                else:
                    ins.then_inc(S("conv_s"), 1)
            pool.wait_ge(S("conv_s"), 1)
            after_read(pool, "in", "x", XC_N - 1)
            link(pool.tensor_copy(xb_seq[:, :, :, SH:], xs[:, :, :].rearrange("p c (b t) -> p c b t", b=NB)))
            acc = xc[:, :, TP:T].rearrange("p c (b t) -> p c b t", b=NB)
            tmp4 = tmp.rearrange("p (c b t) -> p c b t", c=XC_N, b=NB)
            pool.wait_ge(S("u_out"), 16 * (1 + NB))
            link(pool.tensor_tensor(acc, xb_seq[:, :, :, 0:TB], w4(spar, 0, XC_N), ALU.mult))
            link(pool.tensor_tensor(acc, acc, w4(spar, SW, XC_N), ALU.add))
            for k in range(1, SW):
                link(pool.tensor_tensor(tmp4, xb_seq[:, :, :, k:k + TB], w4(spar, k, XC_N), ALU.mult))
                ins = pool.tensor_tensor(acc, acc, tmp4, ALU.add)
                if k < SW - 1:
                    link(ins)
                else:
                    ins.then_inc(S("xconv_s"), 1)
            pool.wait_ge(S("xconv_s"), 1)

            pool.wait_ge(S("x_out"), 16 * (1 + SH))
            for r, (t0, n) in enumerate(TILES):
                sg = seg if r < 2 else segs
                pool.wait_ge(S("dte"), r + 1)
                after_read(pool, "xT", r, 1)
                if r > 0:
                    pool.wait_ge(filled, J[("st", r - 1, 1)] + 1)
                pool.tensor_tensor(xw[0:n, :].rearrange("p (h c) -> p h c", h=H),
                                   xdt[0:n, r, :].rearrange("p (h c) -> p h c", h=H),
                                   bc(dte[0:n, :].unsqueeze(2), [n, H, HD]), ALU.mult).then_inc(S("xw"), 1)
                after_read(pool, "cb", r)
                pool.wait_ge(S("segexp"), 4 * r + 4)
                pool.tensor_tensor(sg[0:n, 12:16, :], sg[0:n, 12:16, :], bc(cbm[0:n, 1:2, 0:n], [n, 4, n]),
                                   ALU.mult).then_inc(S("mdone_pool"), 1)

            pool.wait_ge(S("gated"), 1)
            pool.dma_start(wr[:, :, 0:NG], A["router_group_w"][0].rearrange("(p k) n -> p k n", k=KD))\
                .then_inc(S("wr_in"), 16)
            for g in range(NG):
                pool.dma_start(wr[:, :, NG + EG * g:NG + EG * g + EG],
                               A["router_expert_w"][0, g].rearrange("(p k) n -> p k n", k=KD))\
                    .then_inc(S("wr_in"), 16)
            pool.dma_start(rbias[:, 0:NG], A["router_group_b"].to_broadcast([P, NG])).then_inc(S("wr_in"), 16)
            pool.dma_start(rbias[:, NG:], A["router_expert_b"].rearrange("a g e -> a (g e)").to_broadcast([P, NE]))\
                .then_inc(S("wr_in"), 16)

            pool.wait_ge(S("y_done"), 1)
            pool.iota(slotno[:, :].rearrange("p (a s) -> p a s", a=2), [[0, 2], [1, CAP]], base=0,
                      channel_multiplier=0, allow_small_or_imprecise_dtypes=True)
            pool.iota(desc4, [[-1, NG]], base=NG, channel_multiplier=0, allow_small_or_imprecise_dtypes=True)
            pool.iota(desc8, [[-1, EG]], base=EG, channel_multiplier=0, allow_small_or_imprecise_dtypes=True)
            pool.iota(tokid, [[P, 3]], base=0, channel_multiplier=1, allow_small_or_imprecise_dtypes=True)
            link(pool.memset(halfrow, 2 * BIG))
            link(pool.memset(halfrow[CAP:P, :], 2 * BIG + 1))
            pool.memset(gidx, int(BIG))
            pool.memset(sidx, int(2 * BIG)).then_inc(S("rconst"), 1)
            pool.wait_ge(filled, J[("outs",)] + 1)
            link(pool.memset(gat[1], 0.0))
            pool.wait_ge(S("rinv"), 1)
            for r, (t0, n) in enumerate(TILES):
                pool.tensor_tensor(hn[0:n, r, :], xt[0:n, r, :], bc(rst[0:n, 3 + r:4 + r], [n, D]), ALU.mult)\
                    .then_inc(S("hn"), 1)

            pool.wait_ge(S("hn_out"), 48)
            pool.wait_ge(S("idx"), 1)

            def carry_wait(w):
                pool.tensor_tensor(wait_word[:, w:w + 1], halfrow, halfrow, ALU.add)

            def gather_dma(b):
                pool.indirect_dma_start(gat[b], None, hn_dram[:, :],
                                        bass.IndirectOffsetOnAxis(ap=gcur[b][0:CAP, 0:1], axis=0),
                                        bounds_check=T - 1, oob_is_err=False).then_inc(S(f"gath{b}"), 16)

            def scatter_dma(b, sem):
                pool.indirect_dma_start(ye_dram[:, :], bass.IndirectOffsetOnAxis(ap=scur[b][:, 0:1], axis=0),
                                        yo[b], None, bounds_check=4 * T - 1, oob_is_err=False)\
                    .then_inc(sem, 16)

            pool.tensor_copy(gcur[1], gidx[:, 1:2]).then_inc(S("cur"), 1)
            pool.wait_ge(S("cur"), 1)
            gather_dma(1)

            def expert(i, b):
                e = 2 * i + b
                pool.wait_ge(S("xg_T"), e + 1)
                pool.tensor_copy(gcur[b], gidx[:, bass.ds(e + 2, 1)])
                wait(pool, S(f"scat{b}"), 16 * i)
                pool.tensor_copy(scur[b], sidx[:, bass.ds(e, 1)]).then_inc(S("cur"), 1)
                pool.wait_ge(S("cur"), e + 2)
                carry_wait(0)
                gather_dma(b)
                pool.wait_ge(S("yo"), e + 1)
                carry_wait(1)
                scatter_dma(b, S(f"scat{b}"))

            for b in range(2):
                expert(0, b)
            with pool.Fori(1, NE // 2) as i:
                for b in range(2):
                    expert(i, b)
            pool.wait_ge(S("gath0"), 16 * (NE // 2))
            pool.wait_ge(S("gath1"), 16 * (NE // 2 + 1))
            for b in range(2):
                pool.wait_ge(S(f"scat{b}"), 16 * NE // 2)
            over = pool.value_load(mcount[0:1, 0:1], min_val=0, max_val=T)
            with pool.If(over > CAP):
                pool.memset(gat[0], 0.0).then_inc(S("sl_next"), 1)
                with pool.Fori(0, MAXPASS - 1) as q:
                    pool.wait_ge(S("sl_idx"), q + 1)
                    carry_wait(2)
                    with pool.Fori(0, NE) as e:
                        n = q * NE + e
                        pool.tensor_copy(gcur[0], gidx[:, bass.ds(e, 1)]).then_inc(S("sl_cur"), 1)
                        pool.tensor_copy(scur[0], sidx[:, bass.ds(e, 1)]).then_inc(S("sl_cur"), 1)
                        pool.wait_ge(S("sl_cur"), 2 * n + 2)
                        carry_wait(3)
                        pool.indirect_dma_start(gat[0], None, hn_dram[:, :],
                                                bass.IndirectOffsetOnAxis(ap=gcur[0][0:CAP, 0:1], axis=0),
                                                bounds_check=T - 1, oob_is_err=False).then_inc(S("sl_g"), 16)
                        pool.wait_ge(S("sl_y"), n + 1)
                        carry_wait(4)
                        scatter_dma(0, S("sl_sc"))
                        pool.wait_ge(S("sl_sc"), 16 * (n + 1))
                        carry_wait(5)
                        pool.memset(gcur[1], 0).then_inc(S("sl_next"), 1)
            pool.memset(gat[0], 0.0).then_inc(S("ye_all"), 1)

        @block.tensor
        def _(pe):
            pe.wait_ge(S("ident"), 1)
            for r, (t0, n) in enumerate(TILES):
                pe.wait_ge(S("xn"), r + 1)
                for q in range(2):
                    pt = take(pe, "xt", r, q)
                    for k in range(4):
                        ins = pe.transpose(pt[:, P * k:P * k + n], xt[0:n, r, 4 * q + k:D:KD], ident[0:n, 0:n])
                    ins.then_inc(filled, 1)
            pe.wait_ge(*read_of(("xt", 2, 1)))

            def project(name, unit, c):
                pt = take(pe, *name)
                if unit is None:
                    w, m = wdt, H
                else:
                    w, m = landed(pe, unit).rearrange("p (k c) -> p k c", k=KD)[:, :, P * c:P * c + P], P
                for k in range(KD):
                    ins = pe.matmul(pt[0:m, 0:T], w[:, k, :], ht[:, k, :], start=k == 0, stop=k == KD - 1)
                ins.then_inc(filled, 1)

            def parameters_T():
                pe.wait_ge(S("par_in"), 16 * 10)
                pt = take(pe, "par")
                for c in range(NC):
                    ins = pe.transpose(pt[:, N_PAR * c:N_PAR * (c + 1)], pst[:, P * c:P * c + P],
                                       ident[0:N_PAR, 0:N_PAR])
                ins.then_inc(filled, 1)
                pt = take(pe, "spar")
                for c in range(XC_N):
                    pe.transpose(pt[:, 5 * c:5 * c + 5], sst[:, P * c:P * c + P], ident[0:5, 0:5])
                    ins = pe.transpose(pt[:, 60 + 24 * c:84 + 24 * c], sstate[:, P * c:P * c + P], ident[0:24, 0:24])
                ins.then_inc(filled, 1)
                for h in range(2):
                    for q in range(2):
                        pt = take(pe, "cst", h, q)
                        for c in range(4):
                            cc = 4 * q + c
                            ins = pe.transpose(pt[:, 120 * c:120 * c + 120], cstate[h][:, P * cc:P * cc + P],
                                               ident[0:120, 0:120])
                        ins.then_inc(filled, 1)

            for c in range(NC):
                project(("in", "b", c), f"ub{c // 4}", c % 4)
                if c == 0:
                    parameters_T()
                project(("in", "a", c), f"ua{c // 4}", c % 4)
            pe.wait_ge(S("wdt_in"), 16)
            project(("in", "dt", 0), None, 0)
            for c in range(XC_N):
                project(("in", "x", c), f"x{c // 4}", c % 4)
                if c == 0:
                    after_read(pe, "in", "dt", 0)
                    pt = take(pe, "dtT")
                    for r, (t0, n) in enumerate(TILES):
                        ins = pe.transpose(pt[0:n, H * r:H * r + H], dtr[:, t0:t0 + n], ident[0:H, 0:H])
                    ins.then_inc(filled, 1)
                if c == 1:
                    pe.wait_ge(S("glu"), NC)
                    for q in range(2):
                        pt = take(pe, "ut", q)
                        for k in range(4):
                            ins = pe.transpose(pt[0:HIST, P * k:P * k + P], u[:, 4 * q + k, TP:TP + HIST],
                                               ident[:, :])
                        ins.then_inc(filled, 1)
                    for q in range(2):
                        pt = take(pe, "us", q)
                        for k in range(4):
                            ins = pe.transpose(pt[0:TS, P * k:P * k + P], usc[:, 4 * q + k, :], ident[:, :])
                        ins.then_inc(filled, 1)
            for c in range(NC):
                project(("in", "z", c), f"z{c // 4}", c % 4)
                if c == 1:
                    after_read(pe, "in", "x", XC_N - 1)
                    for q in range(3):
                        pt = take(pe, "xtail", q)
                        for k in range(4):
                            ins = pe.transpose(pt[0:SH, P * k:P * k + P], xb[:, 4 * q + k, TP:TP + SH], ident[:, :])
                        ins.then_inc(filled, 1)
                    for q in range(3):
                        pt = take(pe, "xs", q)
                        for k in range(4):
                            ins = pe.transpose(pt[0:TS, P * k:P * k + P], xs[:, 4 * q + k, :], ident[:, :])
                        ins.then_inc(filled, 1)

            pe.wait_ge(S("conv"), NC)
            pe.wait_ge(S("conv_s"), 1)
            pe.wait_ge(S("conv_s2"), 1)
            pt = take(pe, "mean")
            for c in range(NC):
                ins = pe.matmul(pt[:, 0:T], ones[:, :], vv[:, c, :], start=c == 0, stop=c == NC - 1)
            ins.then_inc(filled, 1)

            pe.wait_ge(S("xact"), 1)
            for r, (t0, n) in enumerate(TILES):
                m_tri, m_later = (tri, later) if r < 2 else (trib, laterb)
                tt = toks(r)
                for q in range(2):
                    pt = take(pe, "xT", r, q)
                    for k in range(4):
                        ins = pe.transpose(pt[0:n, P * k:P * k + P], xc[:, 4 * q + k, tt], ident[:, :])
                    ins.then_inc(filled, 1)
                pt = take(pe, "bT", r)
                for g in range(G):
                    ins = pe.transpose(pt[0:n, P * g:P * g + P], xc[:, NC + g, tt], ident[:, :])
                ins.then_inc(filled, 1)
                pe.wait_ge(S("dta"), 1)
                pt = take(pe, "acum", r)
                pe.matmul(pt[0:n, 0:H], m_tri[0:n, 0:n], dta[0:n, r, :], start=True, stop=True)
                pe.matmul(pt[0:n, H:2 * H], m_later[0:n, 0:n], dta[0:n, r, :], start=True, stop=True)\
                    .then_inc(filled, 1)
                pt = take(pe, "cb", r)
                for g in range(G):
                    ins = pe.matmul(pt[0:n, P * g:P * g + n], xc[:, NC + g, tt], xc[:, NC + G + g, tt],
                                    start=True, stop=True)
                ins.then_inc(filled, 1)
                for q in range(4):
                    pt = take(pe, "seg", r, q)
                    for k in range(4):
                        ins = pe.matmul(pt[0:n, n * k:n * k + n], bc(dta[0:n, r, 4 * q + k:4 * q + k + 1], [n, n]),
                                        m_tri[0:n, 0:n], start=True, stop=True)
                    ins.then_inc(filled, 1)
                if r == 0:
                    pe.wait_ge(S("vsq"), 1)
                    pt = take(pe, "var")
                    for c in range(NC):
                        ins = pe.matmul(pt[:, 0:T], ones[:, :], yt[:, c, :], start=c == 0, stop=c == NC - 1)
                    ins.then_inc(filled, 1)
                if r > 0:
                    per = 4 if r < 2 else 8
                    for q in range(NC // per):
                        pt = take(pe, "eb", r, q)
                        for k in range(per):
                            for hh in range(2):
                                hd = 2 * (per * q + k) + hh
                                ins = pe.matmul(pt[64 * hh:64 * hh + 64, n * k:n * k + n],
                                                bc(dta[0:n, r, hd:hd + 1], [n, HD]), m_tri[0:n, 0:n],
                                                start=True, stop=True)
                        ins.then_inc(filled, 1)
                if r == 1:
                    after_read(pe, "st", 0, 1)
                    for q in range(2):
                        pt = take(pe, "hpT", q)
                        for k in range(4):
                            ins = pe.transpose(pt[:, P * k:P * k + P], hp[:, 4 * q + k, :], ident[:, :])
                        ins.then_inc(filled, 1)
                    after_read(pe, "hpT", 1)
                    for q in range(2):
                        pt = take(pe, "yo", q)
                        for k in range(4):
                            ins = pe.matmul(pt[:, P * k:P * k + P], hpt[:, 4 * q + k, :],
                                            xc[:, NC + G + q, tt], start=True, stop=True)
                        ins.then_inc(filled, 1)
                pe.wait_ge(S("mdone"), r + 1)
                pe.wait_ge(S("mdone_pool"), r + 1)
                if r < 2:
                    for q in range(2):
                        pt = take(pe, "yd", r, q)
                        for k in range(4):
                            for hh in range(2):
                                hd = 2 * (4 * q + k) + hh
                                ins = pe.matmul(pt[64 * hh:64 * hh + 64, P * k:P * k + P],
                                                xdt[:, r, HD * hd:HD * hd + HD], seg[:, hd, :],
                                                start=True, stop=True)
                        ins.then_inc(filled, 1)
                    pe.wait_ge(S("xw"), r + 1)
                    for q in range(2):
                        pt = take(pe, "st", r, q)
                        for k in range(4):
                            c = 4 * q + k
                            ins = pe.matmul(pt[:, P * k:P * k + P], xw[:, P * c:P * c + P],
                                            bt[:, r, NS * q:NS * q + NS], start=True, stop=True)
                        ins.then_inc(filled, 1)
            pt = take(pe, "yds")
            for k in range(NC):
                for hh in range(2):
                    hd = 2 * k + hh
                    ins = pe.matmul(pt[64 * hh:64 * hh + 64, TS * k:TS * k + TS],
                                    xdt[0:TS, 2, HD * hd:HD * hd + HD], segs[:, hd, :], start=True, stop=True)
            ins.then_inc(filled, 1)
            pe.wait_ge(S("xw"), 3)
            pe.wait_ge(S("bm"), 1)

            def states_T(c):
                pe.wait_ge(S(f"h0_in{c}"), 16)
                for q in range(2):
                    pt = take(pe, "h0T", c, q)
                    for k in range(4):
                        ins = pe.transpose(pt[:, P * k:P * k + P], h0[c][:, 4 * q + k, :], ident[:, :])
                    ins.then_inc(filled, 1)

            for c in range(NC):
                g = c // 4
                if c == 0:
                    states_T(0)
                if c + 1 < NC:
                    states_T(c + 1)
                for q in range(2):
                    pt = take(pe, "sts", c, q)
                    pe.matmul(pt[:, :].rearrange("p (b n) -> p b n", b=4),
                              xw[0:TS, P * c:P * c + P], bm[:, 4 * q:4 * q + 4, NS * g:NS * g + NS],
                              start=True, stop=True)\
                        .then_inc(filled, 1)
                after_read(pe, "h0T", c, 1)
                pt = take(pe, "yos", c)
                for b in range(NB):
                    ins = pe.matmul(pt[:, TB * b:TB * b + TB], h0t[c % 2][:, b, :],
                                    xc[:, NC + G + g, TP + TB * b:TP + TB * b + TB], start=True, stop=True)
                ins.then_inc(filled, 1)

            ob = [take(pe, "out", r, q) for r in range(2) for q in range(2)] + [take(pe, "outs")]

            def out_rows(c, r, q):
                w = landed(pe, f"o{c // 4}").rearrange("p (c n) -> p c n", c=4)[:, c % 4, 512 * q:512 * q + 512]
                mix = vv[:, c, toks(r)] if c < NC else yt[:, c - NC, toks(r)]
                dst = ob[2 * r + q][:, :] if r < 2 else ob[4][64 * q:64 * q + 64, :]
                return pe.matmul(dst, mix, w, start=c == 0, stop=c == 2 * NC - 1)

            def gated_norm():
                pe.wait_ge(S("ysq"), 1)
                for g, name in enumerate(("rms", "rms1")):
                    pt = take(pe, name)
                    for k in range(4):
                        ins = pe.matmul(pt[:, 0:T], ones[:, :], sq[:, 4 * g + k, :], start=k == 0, stop=k == 3)
                    ins.then_inc(filled, 1)

            for c in range(2 * NC - 4):
                if c == 0:
                    pe.wait_ge(S("v_done"), 1)
                if c == NC // 2:
                    gated_norm()
                if c == NC:
                    pe.wait_ge(S("y_done"), 1)
                for r in range(3):
                    for q in range(2):
                        ins = out_rows(c, r, q)
                if c % 4 == 3:
                    ins.then_inc(S("wo_used"), 1)
            for r in range(3):
                for q in range(2):
                    for c in range(2 * NC - 4, 2 * NC):
                        ins = out_rows(c, r, q)
                    if r < 2 or q == 1:
                        ins.then_inc(filled, 1)

            for r, (t0, n) in enumerate(TILES):
                pe.wait_ge(S("x2"), r + 1)
                for q in range(2):
                    pt = take(pe, "h2", r, q)
                    for k in range(4):
                        ins = pe.transpose(pt[:, P * k:P * k + n], xt[0:n, r, 4 * q + k:D:KD], ident[0:n, 0:n])
                    ins.then_inc(filled, 1)
            pe.wait_ge(S("wr_in"), 16 * 7)
            after_read(pe, "h2", 2, 1)
            pt = take(pe, "lg")
            for r, (t0, n) in enumerate(TILES):
                for k in range(KD):
                    ins = pe.matmul(pt[0:n, 36 * r:36 * r + 36], h2t[:, k, t0:t0 + n], wr[:, k, :],
                                    start=k == 0, stop=k == KD - 1)
            ins.then_inc(filled, 1)
            pe.wait_ge(S("chosen"), 1)
            pt = take(pe, "rank")
            for r in range(4):
                for rr in range(min(r, 2) + 1):
                    m = before if rr == r else ones
                    ins = pe.matmul(pt[:, NE * r:NE * r + NE], m[:, :], aa[:, rr, :],
                                    start=rr == 0, stop=rr == min(r, 2))
            ins.then_inc(filled, 1)

            def slot_values(pt):
                for n_, (r, w) in enumerate([(r, w) for r in range(3) for w in range(2)]):
                    n = TILES[r][1]
                    ins = pe.matmul(pt[:, 0:3 * NE], osel[0:n, r, w, :],
                                    val[w][0:n, r, :, :].rearrange("p c e -> p (c e)"), start=n_ == 0, stop=n_ == 5)
                return ins

            pe.wait_ge(S("osel"), 1)
            slot_values(take(pe, "slots")).then_inc(filled, 1)
            after_read(pe, "slots")
            pe.wait_ge(free["act"], len([1 for _, who in JOBS if who == "act"]))

            def tokens_T(b):
                for k in range(KD):
                    ins = pe.transpose(bank[2 + b][:, CAP * k:CAP * k + CAP], gat[b][:, k:D:KD], ident[0:CAP, 0:CAP])
                return ins

            def carry_wait(b):
                pe.transpose(bank[2 + b][:, 0:P], ident[:, :], ident[:, :])

            def gate_up(b, wg, wu):
                for k in range(KD):
                    st = dict(start=k == 0, stop=k == KD - 1)
                    pe.matmul(bank[b][0:CAP, :], xgt[b][:, k, :], wg[:, FE * k:FE * k + FE], **st)
                    ins = pe.matmul(bank[b][CAP:P, :], xgt[b][:, k, :], wu[:, FE * k:FE * k + FE], **st)
                return ins

            def hidden_T(b):
                for k in range(4):
                    ins = pe.transpose(bank[4 + b][:, CAP * k:CAP * k + CAP], hid[b][:, k:FE:4], ident[0:CAP, 0:CAP])
                return ins

            def down(b, wd):
                for k in range(4):
                    for q in range(2):
                        ins = pe.matmul(bank[6 + b][CAP * q:CAP * q + CAP, :], hidt[b][:, k, :],
                                        wd[:, D * k + 512 * q:D * k + 512 * q + 512], start=k == 0, stop=k == 3)
                return ins

            pe.wait_ge(S("sel0"), 1)
            pe.wait_ge(S("hn"), 3)
            for r, (t0, n) in enumerate(TILES):
                for q in range(2):
                    ins = pe.matmul(bank[2][CAP * q:CAP * q + CAP, :], sel0[0:n, r, :], hn[0:n, r, 512 * q:512 * q + 512],
                                    start=r == 0, stop=r == 2)
            ins.then_inc(S("picked"), 1)
            pe.wait_ge(S("first_rows"), 1)
            tokens_T(0).then_inc(S("xg_T"), 1)

            def expert(i, b, last=False):
                e = 2 * i + b
                m = [u_slot[3 * b + j] for j in range(3)]
                gate = last_gate if last else ring[:, m[0], :]
                if last:
                    pe.wait_ge(S("last_gate_in"), 16)
                else:
                    pe.wait_ge(ring_in[m[0]], 16 * (slot_pre[m[0]] + 1) + 16 * i)
                pe.wait_ge(ring_in[m[1]], 16 * (slot_pre[m[1]] + 1) + 16 * i)
                pe.wait_ge(S("xgt"), e + 1)
                wait(pe, S("hid"), e - 1)
                gate_up(b, gate, ring[:, m[1], :]).then_inc(S("gu_done"), 1)
                pe.wait_ge(S(f"gath{1 - b}"), 16 * (i + 1))
                wait(pe, S("xgt"), e)
                carry_wait(1 - b)
                tokens_T(1 - b).then_inc(S("xg_T"), 1)
                wait_apart(pe, S("hid"), e + 1)
                wait(pe, S("hidt"), e - 1)
                hidden_T(b).then_inc(S("hid_T"), 1)
                pe.wait_ge(ring_in[m[2]], 16 * (slot_pre[m[2]] + 1) + 16 * i)
                pe.wait_ge(S("hidt"), e + 1)
                wait(pe, S("yo"), e - 1)
                down(b, ring[:, m[2], :]).then_inc(S("dn_done"), 1)

            for b in range(2):
                expert(0, b)
            with pe.Fori(1, NE // 2 - 1) as i:
                for b in range(2):
                    expert(i, b)
            for b in range(2):
                expert(NE // 2 - 1, b, last=b == 1)
            over = pe.value_load(mcount[0:1, 0:1], min_val=0, max_val=T)
            with pe.If(over > CAP):
                pe.wait_ge(S("xgt"), NE + 1)
                pe.wait_ge(S("yo"), NE)
                with pe.Fori(0, MAXPASS - 1) as q:
                    pe.wait_ge(S("sl_osel"), q + 1)
                    slot_values(bank[0]).then_inc(S("sl_slots"), 1)
                    wait_apart(pe, S("sl_idx"), q + 1)
                    with pe.Fori(0, NE) as e:
                        n = q * NE + e
                        pe.wait_ge(S("sl_g"), 16 * (n + 1))
                        carry_wait(0)
                        tokens_T(0).then_inc(S("sl_xT"), 1)
                        pe.wait_ge(S("sl_x"), n + 1)
                        pe.wait_ge(S("sl_w"), 48 * (n + 1))
                        gate_up(0, ring[:, 0, :], ring[:, 1, :]).then_inc(S("sl_gu"), 1)
                        wait_apart(pe, S("sl_hid"), n + 1)
                        hidden_T(0).then_inc(S("sl_hT"), 1)
                        pe.wait_ge(S("sl_hidt"), n + 1)
                        down(0, ring[:, 2, :]).then_inc(S("sl_dn"), 1)

        @block.scalar
        def _(act):
            act.wait_ge(S("eps"), 1)
            for r, (t0, n) in enumerate(TILES):
                act.wait_ge(S(f"x_in{r}"), 16)
                act.activation(yf[0:n, D:2 * D], xt[0:n, r, :], ACT.Square, accum_out=ssq[0:n, r:r + 1])\
                    .then_inc(S("sq"), 1)
                act.wait_ge(S("sq"), r + 1)
            act.activation(rst[:, 0:3], ssq[:, 0:3], ACT.Sqrt, scale=1.0 / D, bias=ssq[:, 7:8]).then_inc(S("rt"), 1)
            ld = lambda dst, src: act.dma_start(dst, src).then_inc(S("ssm_in"), 16)
            row = lambda name, n: A[name][0:1, :].to_broadcast([P, n])
            ld(dtb[:, :], row("ssm_dt_bias", H))
            ld(alog[:, :], row("ssm_a_log", H))
            for hh in range(2):
                ld(dsk[64 * hh:64 * hh + 64, :], A["ssm_d"][0:1, hh:H:2].to_broadcast([HD, NC]))
            ld(lnffn[:, :], A["ln_ffn"].rearrange("a (p k) -> (a p) k", k=KD))
            act.dma_start(O["new_conf_conv_sample"][0, :, 0:HIST - TB, :], A["state_conf_conv"][0, :, TB:HIST, :])\
                .then_inc(S("keep_out"), 16)

            pt = got(act, "in", "b", 0)
            act.activation(sig[0], pt[:, 0:T], ACT.Sigmoid).then_inc(free["act"], 1)
            pt = got(act, "par")
            act.activation(par[:, :, :].rearrange("p c r -> p (c r)"), pt[:, 0:NC * N_PAR], ACT.Copy)\
                .then_inc(free["act"], 1)
            pt = got(act, "spar")
            act.activation(spar[:, :, :].rearrange("p c r -> p (c r)"), pt[:, 0:60], ACT.Copy)
            act.wait_ge(S("consts"), 1)
            for c in range(XC_N):
                ins = act.activation(xb_seq[:, c, :, 0:SH],
                                     pt[:, 60 + 24 * c:84 + 24 * c].rearrange("p (b t) -> p b t", b=NB), ACT.Copy)
            ins.then_inc(free["act"], 1)
            for h in range(2):
                for q in range(2):
                    pt = got(act, "cst", h, q)
                    for c in range(4):
                        ins = act.activation(u_seq[:, 4 * q + c, 4 * h:4 * h + 4, 0:HIST],
                                             pt[:, 120 * c:120 * c + 120].rearrange("p (b t) -> p b t", b=4), ACT.Copy)
                    ins.then_inc(free["act"], 1)

            act.dma_start(wdt, w_in[:, :, C_DT:C_DT + H]).then_inc(S("wdt_in"), 16)
            for c in range(NC):
                b = c % 2
                if c > 0:
                    pt = got(act, "in", "b", c)
                    if c >= 2:
                        act.wait_ge(S("glu"), c - 1)
                    act.activation(sig[b], pt[:, 0:T], ACT.Sigmoid).then_inc(free["act"], 1)
                pt = got(act, "in", "a", c)
                act.activation(uac[b], pt[:, 0:T], ACT.Copy).then_inc(free["act"], 1)
            pt = got(act, "in", "dt", 0)
            act.wait_ge(S("glu"), NC)
            act.activation(dtr, pt[0:H, 0:T], ACT.Copy).then_inc(free["act"], 1)

            def rows_out(dst, pt, q):
                act.activation(dst[:, 512 * q:512 * q + 512], pt[0:dst.shape[0], :], ACT.Copy)\
                    .then_inc(free["act"], 1)

            for c in range(XC_N):
                pt = got(act, "in", "x", c)
                act.activation(xb[:, c, SH:SH + TP], pt[:, 0:TP], ACT.Copy)
                act.activation(xs[:, c, :], pt[:, TP:T], ACT.Copy).then_inc(free["act"], 1)
                if c == 0:
                    pt = got(act, "dtT")
                    for r in range(3):
                        n = TILES[r][1]
                        ins = act.activation(dtk[0:n, r, :], pt[0:n, H * r:H * r + H], ACT.Copy)
                    ins.then_inc(free["act"], 1)
                if c == 1:
                    for q in range(2):
                        rows_out(ut_rows, got(act, "ut", q), q)
                    for q in range(2):
                        rows_out(us_rows, got(act, "us", q), q)
                    after_read(act, "us", 1)
                    act.dma_start(O["new_conf_conv_prompt"][0, 0], ut_rows).then_inc(S("u_out"), 16)
                    for b in range(NB):
                        act.dma_start(O["new_conf_conv_sample"][0, b, HIST - TB:HIST, :],
                                      us_rows[TB * b:TB * b + TB, :]).then_inc(S("u_out"), 16)
            for c in range(NC):
                pt = got(act, "in", "z", c)
                act.activation(zz[:, c, :], pt[:, 0:T], ACT.Silu).then_inc(free["act"], 1)
                if c == 1:
                    for q in range(3):
                        rows_out(xtail_rows, got(act, "xtail", q), q)
                    for q in range(3):
                        rows_out(xs_rows, got(act, "xs", q), q)
                    after_read(act, "xs", 2)
                    act.dma_start(O["new_ssm_conv_prompt"][0, 0], xtail_rows).then_inc(S("x_out"), 16)
                    for t in range(SH):
                        act.dma_start(O["new_ssm_conv_sample"][0, :, t, :], xs_rows[TB - SH + t:TS:TB, :])\
                            .then_inc(S("x_out"), 16)

            act.wait_ge(S("xconv"), XC_N)
            act.wait_ge(S("xconv_s"), 1)
            for q in range(3):
                v = xc[:, 4 * q:4 * q + 4, :]
                ins = act.activation(v, v, ACT.Silu)
            ins.then_inc(S("xact"), 1)
            act.activation(alog[:, :], alog[:, :], ACT.Exp)
            act.wait_ge(S("dt_abs"), 1)
            act.activation(sp[:, 1, :], sp[:, 0, :], ACT.Exp, scale=-1.0).then_inc(S("dt_exp"), 1)
            act.wait_ge(S("v_mean"), 1)
            act.wait_ge(S("x_out"), 16 * (1 + SH))
            act.activation(yt[:, :, :], vv[:, :, :], ACT.Square).then_inc(S("vsq"), 1)
            c4 = lambda t: t[:, :].rearrange("p (c i) -> p c i", c=4)
            for r, (t0, n) in enumerate(TILES):
                after_read(act, "acum", r)
                if r > 0:
                    act.wait_ge(S("xw"), r)
                act.activation(dte[0:n, :], na[0:n, H:2 * H], ACT.Exp, scale=-1.0).then_inc(S("dte"), 1)
                v = seg if r < 2 else segs
                for q in range(4):
                    after_read(act, "seg", r, q)
                    act.activation(v[0:n, 4 * q:4 * q + 4, :], v[0:n, 4 * q:4 * q + 4, :], ACT.Exp)\
                        .then_inc(S("segexp"), 1)
                if r == 0:
                    pt = got(act, "var")
                    act.activation(yt[:, 0, :], pt[:, 0:T], ACT.Sqrt, scale=1.0 / D, bias=ssq[:, 7:8])\
                        .then_inc(free["act"], 1)
                    act.wait_ge(S("v_norm"), 1)
                    for q in range(2):
                        act.activation(yt[:, 4 * q:4 * q + 4, toks(0)], c4(got(act, "yd", 0, q)), ACT.Copy)\
                            .then_inc(free["act"], 1)
                    for q in range(2):
                        act.activation(hp[:, 4 * q:4 * q + 4, :], c4(got(act, "st", 0, q)), ACT.Copy)\
                            .then_inc(free["act"], 1)
                if r == 1:
                    for q in range(2):
                        pt = got(act, "eb", r, q)
                        act.activation(eb[:, 4 * q:4 * q + 4, :], pt[:, :].rearrange("p (c i) -> p c i", c=4), ACT.Exp)\
                            .then_inc(free["act"], 1)
                    for q in range(2):
                        pt = got(act, "hpT", q)
                        act.activation(hpt[:, 4 * q:4 * q + 4, :], pt[:, :].rearrange("p (c i) -> p c i", c=4),
                                       ACT.Copy).then_inc(free["act"], 1)
                if r == 2:
                    act.wait_ge(S("hp_done"), 1)
                    pt = got(act, "eb", r, 0)
                    act.activation(ebs, pt[:, :].rearrange("p (c i) -> p c i", c=NC), ACT.Exp)\
                        .then_inc(free["act"], 1)
            for c in range(NC):
                ins = act.activation(vv[:, c, :], vv[:, c, :], ACT.Silu, scale=par[:, c, R_LNG:R_LNG + 1],
                                     bias=par[:, c, R_LNB:R_LNB + 1])
            ins.then_inc(S("v_done"), 1)
            act.wait_ge(S("hp_out"), 16)
            for c in range(NC):
                if c >= 2:
                    act.wait_ge(filled, J[("yos", c - 2)] + 1)
                for q in range(2):
                    pt = got(act, "h0T", c, q)
                    act.activation(h0t[c % 2][:, 4 * q:4 * q + 4, :], pt[:, :].rearrange("p (b n) -> p b n", b=4),
                                   ACT.Copy).then_inc(free["act"], 1)
            act.wait_ge(S("gated"), 1)
            act.activation(sq, yt[:, :, :], ACT.Square).then_inc(S("ysq"), 1)
            for g, name in enumerate(("rms", "rms1")):
                pt = got(act, name)
                act.activation(rs[:, g, :], pt[:, 0:T], ACT.Sqrt, scale=1.0 / (D // G), bias=ssq[:, 7:8])\
                    .then_inc(free["act"], 1)

            for r, (t0, n) in enumerate(TILES):
                act.wait_ge(S("x2"), r + 1)
                act.activation(xcf[0:n, 0:D], xt[0:n, r, :], ACT.Square, accum_out=ssq[0:n, r:r + 1])\
                    .then_inc(S("sq2"), 1)
                act.wait_ge(S("sq2"), r + 1)
            act.activation(rst[:, 0:3], ssq[:, 0:3], ACT.Sqrt, scale=1.0 / D, bias=ssq[:, 7:8]).then_inc(S("rt2"), 1)
            act.dma_start(gfin, A["ln_final"].rearrange("(a d) -> a d", a=1).to_broadcast([P, D])).then_inc(S("gfin_in"), 16)
            for r, (t0, n) in enumerate(TILES):
                act.wait_ge(S("hn"), r + 1)
                act.dma_start(hn_dram[t0:t0 + n, :], hn[0:n, r, :]).then_inc(S("hn_out"), 16)
            act.wait_ge(S("g_in"), 1)
            act.activation(sg4[:, :, :], sg4[:, :, :], ACT.Exp).then_inc(S("g_exp"), 1)
            act.wait_ge(S("e_in"), 1)
            act.activation(cols[:, M_E, :], cols[:, M_T, :], ACT.Exp).then_inc(S("e_exp"), 1)

            def expert(i, b):
                e = 2 * i + b
                act.wait_ge(S("gu_done"), e + 1)
                wait(act, S("hid"), e - 1)
                act.activation(sil[b], bank[b][0:CAP, :], ACT.Silu).then_inc(S("sil"), 1)
                act.wait_ge(S("hid_T"), e + 1)
                wait(act, S("dn_done"), e - 1)
                act.activation(hidt[b], bank[4 + b][:, 0:4 * CAP].rearrange("p (k s) -> p k s", k=4), ACT.Copy)\
                    .then_inc(S("hidt"), 1)

            for b in range(2):
                expert(0, b)
            with act.Fori(1, NE // 2) as i:
                for b in range(2):
                    expert(i, b)
            over = act.value_load(mcount[0:1, 0:1], min_val=0, max_val=T)
            with act.If(over > CAP):
                with act.Fori(0, MAXPASS - 1) as q:
                    with act.Fori(0, NE) as e:
                        n = q * NE + e
                        act.wait_ge(S("sl_gu"), n + 1)
                        act.activation(sil[0], bank[0][0:CAP, :], ACT.Silu).then_inc(S("sl_sil"), 1)
                        act.wait_ge(S("sl_hT"), n + 1)
                        act.activation(hidt[0], bank[4][:, 0:4 * CAP].rearrange("p (k s) -> p k s", k=4), ACT.Copy)\
                            .then_inc(S("sl_hidt"), 1)
            for r, (t0, n) in enumerate(TILES):
                act.wait_ge(S("x3"), r + 1)
                act.activation(yf[0:n, D:2 * D], xt[0:n, r, :], ACT.Square, accum_out=ssq[0:n, r:r + 1])\
                    .then_inc(S("sq3"), 1)
                act.wait_ge(S("sq3"), r + 1)
                act.activation(rst[:, r:r + 1], ssq[:, r:r + 1], ACT.Sqrt, scale=1.0 / D, bias=ssq[:, 7:8])\
                    .then_inc(S("rt3"), 1)
            act.wait_ge(S("keep_out"), 16)
            act.wait_ge(S("u_out"), 16 * (1 + NB))

        @block.vector
        def _(dve):
            own = [0]

            def link(ins):
                own[0] += 1
                ins.then_inc(S("dve_own"), 1)
                dve.wait_ge(S("dve_own"), own[0])

            tt_ = lambda out, a, b, op: dve.tensor_tensor(out, a, b, op)
            stt = lambda out, a, s_, b, op0, op1: dve.scalar_tensor_tensor(out=out, in0=a, scalar=s_, in1=b,
                                                                           op0=op0, op1=op1)
            dve.wait_ge(S("rt"), 1)
            link(dve.reciprocal(rst[:, 3:6], rst[:, 0:3]))
            for r, (t0, n) in enumerate(TILES):
                dve.tensor_scalar(xt[0:n, r, :], xt[0:n, r, :], rst[0:n, 3 + r:4 + r], None, ALU.mult)\
                    .then_inc(S("xn"), 1)
            dve.wait_ge(S("mix_in"), 16)
            for r, (t0, n) in enumerate(TILES):
                for q in range(2):
                    pt = got(dve, "xt", r, q)
                    v = pt[:, :].rearrange("p (k t) -> p k t", k=4)[:, :, 0:n]
                    tt_(ht[:, 4 * q:4 * q + 4, toks(r)], v,
                        bc(lnmix[:, 4 * q:4 * q + 4].unsqueeze(2), [P, 4, n]), ALU.mult).then_inc(free["dve"], 1)

            def conv(src, dst, w, bias_row, taps, chunks, ready, sem, step):
                n = 0
                for c0 in range(0, chunks, 2):
                    ready(c0 + 1)
                    for k in range(taps):
                        for c in (c0, c0 + 1):
                            v, o = src[:, c, k:k + TP], dst[:, c, 0:TP]
                            if k == 0:
                                ins = dve.tensor_scalar(o, v, w[:, c, 0:1], w[:, c, bias_row:bias_row + 1],
                                                        ALU.mult, ALU.add)
                            else:
                                dve.wait_ge(step, n if k == taps - 1 and c > c0 else n - 1)
                                ins = stt(o, v, w[:, c, k:k + 1], o, ALU.mult, ALU.add)
                            if k < taps - 1:
                                ins.then_inc(step, 1)
                                n += 1
                            else:
                                ins.then_inc(sem, 1)

            after_read(dve, "par")
            conv(u, vv, par, R_DWB, KW, NC, lambda c: dve.wait_ge(S("glu"), c + 1), S("conv"), S("tap"))
            after_read(dve, "dtT")
            dve.wait_ge(S("ssm_in"), 16 * 5)
            dve.wait_ge(S("consts"), 1)
            link(tt_(dtk[:, :, :], dtk[:, :, :], bc(dtb[:, :].unsqueeze(1), [P, 3, H]), ALU.add))
            d48 = dtk[:, :, :].rearrange("p r h -> p (r h)")
            stt(sp[:, 0, :], d48, -1.0, d48, ALU.mult, ALU.max).then_inc(S("dt_abs"), 1)
            dve.wait_ge(S("u_out"), 16 * (1 + NB))
            conv(xb, xc, spar, SW, SW, XC_N, lambda c: after_read(dve, "in", "x", c), S("xconv"), S("xtap"))
            seqs = lambda t, c: t[:, c, TP:T].rearrange("p (b t) -> p b t", b=NB)

            def conv_seqs(src, dst, w, bias_row, taps, chunks, sem, step):
                n = 0
                for k in range(taps):
                    for c in chunks:
                        v, o = src[:, c, :, k:k + TB], seqs(dst, c)
                        if k == 0:
                            ins = dve.tensor_scalar(o, v, w[:, c, 0:1], w[:, c, bias_row:bias_row + 1],
                                                    ALU.mult, ALU.add)
                        else:
                            dve.wait_ge(step, n - len(chunks) + 1)
                            ins = stt(o, v, w[:, c, k:k + 1], o, ALU.mult, ALU.add)
                        ins.then_inc(step, 1)
                        n += 1
                dve.wait_ge(step, n)
                dve.sem_inc(sem, 1)

            dve.wait_ge(filled, J[("us", 1)] + 1)
            after_read(dve, "cst", 1, 1)
            conv_seqs(u_seq, vv, par, R_DWB, KW, range(NC_POOL, NC), S("conv_s2"), S("stap"))

            dve.wait_ge(S("dt_exp"), 1)
            link(dve.tensor_scalar(sp[:, 2, :], sp[:, 1, :], 2.0, None, ALU.add))
            link(dve.reciprocal(sp[:, 2, :], sp[:, 2, :]))
            link(tt_(sp[:, 1, :], sp[:, 1, :], sp[:, 2, :], ALU.mult))
            link(tt_(sp[:, 2, :], sp[:, 1, :], sp[:, 1, :], ALU.mult))
            link(dve.tensor_scalar(sp[:, 3, :], sp[:, 2, :], 1.0 / 17, None, ALU.mult))
            for k in (15, 13, 11, 9, 7, 5, 3):
                link(stt(sp[:, 3, :], sp[:, 3, :], 1.0 / k, sp[:, 2, :], ALU.add, ALU.mult))
            link(stt(sp[:, 3, :], sp[:, 3, :], 1.0, sp[:, 1, :], ALU.add, ALU.mult))
            link(dve.tensor_scalar(sp[:, 4, :], d48, 0.0, None, ALU.max))
            link(stt(d48, sp[:, 3, :], 2.0, sp[:, 4, :], ALU.mult, ALU.add))
            stt(dta[:, :, :], dtk[:, :, :], -1.0, bc(alog[:, :].unsqueeze(1), [P, 3, H]), ALU.mult, ALU.mult)\
                .then_inc(S("dta"), 1)

            pt = got(dve, "mean")
            stt(vv[:, :, :], bc(pt[:, 0:T].unsqueeze(1), [P, NC, T]), -1.0 / D, vv[:, :, :], ALU.mult, ALU.add)\
                .then_inc(free["dve"], 1)
            after_read(dve, "mean")
            dve.sem_inc(S("v_mean"), 1)

            for r, (t0, n) in enumerate(TILES):
                sg, m_tri = (seg, tri) if r < 2 else (segs, trib)
                for q in range(2):
                    pt = got(dve, "xT", r, q)
                    tt_(xdt[0:n, r, 512 * q:512 * q + 512].rearrange("p (h c) -> p h c", h=8),
                        pt[0:n, :].rearrange("p (h c) -> p h c", h=8),
                        bc(dtk[0:n, r, 8 * q:8 * q + 8].unsqueeze(2), [n, 8, HD]), ALU.mult).then_inc(free["dve"], 1)
                pt = got(dve, "bT", r)
                dve.tensor_copy(bt[0:n, r, :], pt[0:n, 0:G * NS]).then_inc(free["dve"], 1)
                pt = got(dve, "acum", r)
                dve.tensor_scalar(na[0:n, :], pt[0:n, 0:2 * H], -1.0, None, ALU.mult).then_inc(free["dve"], 1)
                pt = got(dve, "cb", r)
                tt_(cbm[0:n, :, 0:n], pt[0:n, 0:2 * P].rearrange("p (g i) -> p g i", g=G)[:, :, 0:n],
                    bc(m_tri[0:n, 0:n].unsqueeze(1), [n, G, n]), ALU.mult).then_inc(free["dve"], 1)
                after_read(dve, "cb", r)
                for q in range(4):
                    pt = got(dve, "seg", r, q)
                    for k in range(4):
                        hd = 4 * q + k
                        ins = dve.tensor_scalar(sg[0:n, hd, :], pt[0:n, n * k:n * k + n], na[0:n, hd:hd + 1], 0.0,
                                                ALU.add, ALU.min)
                    ins.then_inc(free["dve"], 1)
                for q in range(3):
                    dve.wait_ge(S("segexp"), 4 * r + q + 1)
                    ins = tt_(sg[0:n, 4 * q:4 * q + 4, :], sg[0:n, 4 * q:4 * q + 4, :],
                              bc(cbm[0:n, q // 2:q // 2 + 1, 0:n], [n, 4, n]), ALU.mult)
                ins.then_inc(S("mdone"), 1)
                if r == 0:
                    after_read(dve, "var")
                    link(dve.reciprocal(yt[:, 0, :], yt[:, 0, :]))
                    tt_(vv[:, :, :], vv[:, :, :], bc(yt[:, 0:1, :], [P, NC, T]), ALU.mult).then_inc(S("v_norm"), 1)
                c4 = lambda t: t[:, :].rearrange("p (c i) -> p c i", c=4)
                if r == 1:
                    after_read(dve, "eb", 1, 1)
                    for q in range(2):
                        pt = got(dve, "yo", q)
                        tt_(yt[:, 4 * q:4 * q + 4, toks(r)], c4(pt), eb[:, 4 * q:4 * q + 4, :], ALU.mult)\
                            .then_inc(free["dve"], 1)
                    after_read(dve, "yo", 1)
                if r == 1:
                    for q in range(2):
                        pt = got(dve, "yd", r, q)
                        v = yt[:, 4 * q:4 * q + 4, toks(r)]
                        tt_(v, v, c4(pt), ALU.add).then_inc(free["dve"], 1)
                    for q in range(2):
                        pt = got(dve, "st", r, q)
                        for k in range(4):
                            c = 4 * q + k
                            ins = stt(hp[:, c, :], hp[:, c, :], eb[:, c, P - 1:P], pt[:, P * k:P * k + P],
                                      ALU.mult, ALU.add)
                        ins.then_inc(free["dve"], 1)
                    after_read(dve, "st", 1, 1)
                    dve.sem_inc(S("hp_done"), 1)
            dve.wait_ge(filled, J[("yd", 1, 1)] + 1)
            tt_(bm, bc(bt[0:TS, 2:3, :], [TS, NB, G * NS]), bc(bmask[:, :].unsqueeze(2), [TS, NB, G * NS]), ALU.mult)\
                .then_inc(S("bm"), 1)
            pt = got(dve, "yds")
            dve.tensor_copy(yt[:, :, TP:T], pt[:, :].rearrange("p (c i) -> p c i", c=NC)).then_inc(free["dve"], 1)
            after_read(dve, "yds")
            after_read(dve, "eb", 2, 0)
            for c in range(NC):
                for q in range(2):
                    pt = got(dve, "sts", c, q)
                    for k in range(4):
                        b = 4 * q + k
                        v = h0[c][:, b, :]
                        ins = stt(v, v, ebs[:, c, TB * b + TB - 1:TB * b + TB], pt[:, P * k:P * k + P],
                                  ALU.mult, ALU.add)
                    ins.then_inc(free["dve"], 1)
                after_read(dve, "sts", c, 1)
                dve.sem_inc(S("h0_new"), 1)
                pt = got(dve, "yos", c)
                if c >= 1:
                    dve.wait_ge(S("dve_own"), own[0])
                tt_(ebs[:, c, :], ebs[:, c, :], pt[:, 0:TS], ALU.mult).then_inc(free["dve"], 1)
                after_read(dve, "yos", c)
                ins = tt_(yt[:, c, TP:T], yt[:, c, TP:T], ebs[:, c, :], ALU.add)
            link(ins)
            for c in range(NC):
                ins = stt(yt[:, c, :], xc[:, c, :], dsk[:, c:c + 1], yt[:, c, :], ALU.mult, ALU.add)
            link(ins)
            tt_(yt[:, :, :], yt[:, :, :], zz[:, :, :], ALU.mult).then_inc(S("gated"), 1)
            for g, name in enumerate(("rms", "rms1")):
                after_read(dve, name)
                link(dve.reciprocal(rs[:, g, :], rs[:, g, :]))
                for k in range(4):
                    c = 4 * g + k
                    ins = stt(yt[:, c, :], yt[:, c, :], par[:, c, R_NG:R_NG + 1], rs[:, g, :], ALU.mult, ALU.mult)
            ins.then_inc(S("y_done"), 1)

            dve.wait_ge(S("x_again"), 48)
            for r in range(2):
                for q in range(2):
                    pt = got(dve, "out", r, q)
                    v = xt[:, r, 512 * q:512 * q + 512]
                    tt_(v, v, pt[:, :], ALU.add).then_inc(free["dve"], 1)
                after_read(dve, "out", r, 1)
                dve.sem_inc(S("x2"), 1)
            pt = got(dve, "outs")
            for q in range(2):
                v = xt[0:TS, 2, 512 * q:512 * q + 512]
                ins = tt_(v, v, pt[64 * q:64 * q + 64, :], ALU.add)
            ins.then_inc(free["dve"], 1)
            after_read(dve, "outs")
            dve.sem_inc(S("x2"), 1)
            for r, (t0, n) in enumerate(TILES):
                for q in range(2):
                    pt = got(dve, "h2", r, q)
                    v = pt[:, :].rearrange("p (k t) -> p k t", k=4)[:, :, 0:n]
                    tt_(h2t[:, 4 * q:4 * q + 4, toks(r)], v,
                        bc(lnffn[:, 4 * q:4 * q + 4].unsqueeze(2), [P, 4, n]), ALU.mult).then_inc(free["dve"], 1)

            dve.wait_ge(S("rt2"), 1)
            dve.reciprocal(rst[:, 3:6], rst[:, 0:3]).then_inc(S("rinv"), 1)
            dve.wait_ge(S("rinv"), 1)
            link(dve.memset(lg[:, :, :], 0.0))
            dve.wait_ge(S("rconst"), 1)
            pt = got(dve, "lg")
            for r, (t0, n) in enumerate(TILES):
                ins = stt(lg[0:n, r, :], pt[0:n, 36 * r:36 * r + 36], rst[0:n, 3 + r:4 + r], rbias[0:n, :],
                          ALU.mult, ALU.add)
            ins.then_inc(free["dve"], 1)
            after_read(dve, "lg")

            def col(n):
                return cols[:, n, :]

            def wide(n, w):
                return bc(cols[:, n, :].unsqueeze(2), [P, 3, w])

            def first_max(vals, w, mx, out, desc, tmp_):
                link(dve.tensor_reduce(col(mx), vals, AX.X, ALU.max))
                link(tt_(tmp_, vals, wide(mx, w), ALU.is_equal))
                link(tt_(tmp_, tmp_, bc(desc.unsqueeze(1), [P, 3, w]), ALU.mult))
                link(dve.tensor_reduce(col(M_T), tmp_, AX.X, ALU.max))
                link(tt_(out, tmp_, wide(M_T, w), ALU.is_equal))

            groups = lg[:, :, 0:NG]
            first_max(groups, NG, M_SSUM, og, desc4, t4)
            tt_(sg4, groups, wide(M_SSUM, NG), ALU.subtract).then_inc(S("g_in"), 1)
            for g in range(NG):
                o = le if g == 0 else t8
                link(tt_(o, lg[:, :, NG + EG * g:NG + EG * g + EG], bc(og[:, :, g:g + 1], [P, 3, EG]), ALU.mult))
                if g:
                    link(tt_(le, le, t8, ALU.add))
            first_max(le, EG, M_M1, o1, desc8, s8)
            link(stt(le, o1, -3.0e38, le, ALU.mult, ALU.add))
            first_max(le, EG, M_M2, o2, desc8, s8)
            tt_(col(M_T), col(M_M2), col(M_M1), ALU.subtract).then_inc(S("e_in"), 1)
            dve.wait_ge(S("g_exp"), 1)
            link(dve.tensor_reduce(col(M_G1), sg4, AX.X, ALU.add))
            link(dve.reciprocal(col(M_G1), col(M_G1)))
            dve.wait_ge(S("e_exp"), 1)
            link(dve.tensor_scalar(col(M_R), col(M_E), 1.0, None, ALU.add))
            link(dve.reciprocal(col(M_R), col(M_R)))
            link(tt_(col(M_W1), col(M_G1), col(M_R), ALU.mult))
            link(tt_(col(M_W2), col(M_W1), col(M_E), ALU.mult))
            for g in range(NG):
                for ee, oo in ((e1, o1), (e2, o2)):
                    ins = tt_(ee[:, :, EG * g:EG * g + EG], oo, bc(og[:, :, g:g + 1], [P, 3, EG]), ALU.mult)
            link(ins)
            for ee in (e1, e2):
                link(dve.memset(ee[TS:P, 2, :], 0.0))
            tt_(aa, e1, e2, ALU.add).then_inc(S("chosen"), 1)
            pt = got(dve, "rank")
            dve.tensor_copy(pos, pt[:, 0:3 * NE].rearrange("p (r n) -> p r n", r=3))
            dve.tensor_copy(cnt, pt[:, 3 * NE:4 * NE]).then_inc(free["dve"], 1)
            after_read(dve, "rank")
            link(dve.tensor_reduce(cols[:, M_T, 0:1], cnt, AX.X, ALU.max))
            dve.tensor_copy(mcount, cols[:, M_T, 0:1]).then_inc(S("count_ready"), 1)
            dve.wait_ge(S("count_ready"), 1)
            for ee, m in ((e1, M_S1), (e2, M_S2)):
                link(tt_(t32, ee, pos, ALU.mult))
                link(dve.tensor_reduce(col(m), t32, AX.X, ALU.add))
            for w, (ee, mw) in enumerate(((e1, M_W1), (e2, M_W2))):
                link(dve.tensor_scalar(col(M_T), tokid.unsqueeze(1)[:, 0, :], -BIG, None, ALU.add))
                tt_(val[w][:, :, 0, :], ee, wide(M_T, NE), ALU.mult)
                link(dve.tensor_scalar(col(M_E), tokid, 2.0, float(w) - BIG, ALU.mult, ALU.add))
                tt_(val[w][:, :, 1, :], ee, wide(M_E, NE), ALU.mult)
                link(tt_(val[w][:, :, 2, :], ee, wide(mw, NE), ALU.mult))

            def slot_select():
                for r in range(3):
                    for w, m in enumerate((M_S1, M_S2)):
                        ins = dve.tensor_scalar(osel[:, r, w, :], slotno, cols[:, m, r:r + 1], None, ALU.is_equal)
                return ins

            def slot_indices(pt):
                dve.tensor_scalar(gidx[:, 0:NE], pt[:, 0:NE], BIG, None, ALU.add)
                dve.tensor_scalar(sidx[:, 0:NE], pt[:, NE:2 * NE], 2.0, halfrow, ALU.mult, ALU.add)
                return dve.tensor_copy(wsl[:, 0:NE], pt[:, 2 * NE:3 * NE])

            slot_select().then_inc(S("osel"), 1)
            dve.wait_ge(S("osel"), 1)
            for r in range(3):
                ins = dve.tensor_scalar(sel0[:, r, :], osel[:, r, 0, 0:CAP], e1[:, r, 0:1], None, ALU.mult)
            link(ins)
            for r in range(3):
                ins = stt(sel0[:, r, :], osel[:, r, 1, 0:CAP], e2[:, r, 0:1], sel0[:, r, :], ALU.mult, ALU.add)
            ins.then_inc(S("sel0"), 1)
            slot_indices(got(dve, "slots")).then_inc(free["dve"], 1)
            after_read(dve, "slots")
            dve.sem_inc(S("idx"), 1)

            def tokens(b):
                return tt_(xgt[b], bank[2 + b][:, :].rearrange("p (k s) -> p k s", k=KD),
                           bc(lnffn[:, :].unsqueeze(2), [P, KD, CAP]), ALU.mult)

            dve.wait_ge(S("picked"), 1)
            for q in range(2):
                ins = dve.tensor_copy(gat[0][:, 512 * q:512 * q + 512], bank[2][CAP * q:CAP * q + CAP, :])
            ins.then_inc(S("first_rows"), 1)
            dve.wait_ge(S("xg_T"), 1)
            tokens(0).then_inc(S("xgt"), 1)

            def expert(i, b):
                e = 2 * i + b
                dve.wait_ge(S("sil"), e + 1)
                wait(dve, S("hid_T"), e - 1)
                tt_(hid[b], sil[b], bank[b][CAP:P, :], ALU.mult).then_inc(S("hid"), 1)
                dve.wait_ge(S("xg_T"), e + 2)
                wait(dve, S("gu_done"), e)
                tokens(1 - b).then_inc(S("xgt"), 1)
                dve.wait_ge(S("dn_done"), e + 1)
                wait(dve, S(f"scat{b}"), 16 * i)
                dve.tensor_scalar(yo[b], bank[6 + b][:, :], wsl[:, bass.ds(e, 1)], None, ALU.mult)\
                    .then_inc(S("yo"), 1)

            for b in range(2):
                expert(0, b)
            with dve.Fori(1, NE // 2) as i:
                for b in range(2):
                    expert(i, b)
            over = dve.value_load(mcount[0:1, 0:1], min_val=0, max_val=T)
            with dve.If(over > CAP):
                dve.wait_ge(S("scat0"), 16 * NE // 2)
                with dve.Fori(0, MAXPASS - 1) as q:
                    dve.wait_ge(S("sl_next"), q * NE + 1)
                    for m in (M_S1, M_S2):
                        ins = dve.tensor_scalar(col(m), col(m), -float(CAP), None, ALU.add)
                    ins.then_inc(S("sl_own"), 1)
                    dve.wait_ge(S("sl_own"), q + 1)
                    slot_select().then_inc(S("sl_osel"), 1)
                    dve.wait_ge(S("sl_slots"), q + 1)
                    slot_indices(bank[0]).then_inc(S("sl_idx"), 1)
                    wait_apart(dve, S("sl_idx"), q + 1)
                    with dve.Fori(0, NE) as e:
                        n = q * NE + e
                        dve.wait_ge(S("sl_xT"), n + 1)
                        tokens(0).then_inc(S("sl_x"), 1)
                        dve.wait_ge(S("sl_sil"), n + 1)
                        tt_(hid[0], sil[0], bank[0][CAP:P, :], ALU.mult).then_inc(S("sl_hid"), 1)
                        dve.wait_ge(S("sl_dn"), n + 1)
                        dve.tensor_scalar(yo[0], bank[6][:, :], wsl[:, bass.ds(e, 1)], None, ALU.mult)\
                            .then_inc(S("sl_y"), 1)

            def add_experts(r):
                n = TILES[r][1]
                dve.wait_ge(S(f"ye_in{r}"), 16)
                link(tt_(xt[0:n, r, :], xt[0:n, r, :], ring[0:n, r, 0:D], ALU.add))
                tt_(xt[0:n, r, :], xt[0:n, r, :], ring[0:n, r, D:2 * D], ALU.add).then_inc(S("x3"), 1)

            def final_norm(r):
                n = TILES[r][1]
                dve.wait_ge(S("rt3"), r + 1)
                link(dve.reciprocal(rst[:, 3 + r:4 + r], rst[:, r:r + 1]))
                stt(xt[0:n, r, :], xt[0:n, r, :], rst[0:n, 3 + r:4 + r], gfin[0:n, :], ALU.mult, ALU.mult)\
                    .then_inc(S("y_final"), 1)

            dve.wait_ge(S("gfin_in"), 16)
            add_experts(0)
            add_experts(1)
            final_norm(0)
            add_experts(2)
            final_norm(1)
            final_norm(2)


_INS = ["x_prompt", "x_sample", "state_conf_conv", "state_ssm_conv", "state_ssm", "ln_mix", "w_in", "conf_dw_w",
        "conf_dw_b", "conf_ln_g", "conf_ln_b", "ssm_conv_w", "ssm_conv_b", "ssm_dt_bias", "ssm_a_log", "ssm_d",
        "ssm_norm_g", "w_out", "ln_ffn", "router_group_w", "router_group_b", "router_expert_w", "router_expert_b",
        "expert_w_gate", "expert_w_up", "expert_w_down", "ln_final"]
_OUTS = [("y_prompt", (1, TP, D)), ("y_sample", (NB, TB, D)), ("new_conf_conv_prompt", (1, 1, HIST, D)),
         ("new_ssm_conv_prompt", (1, 1, SH, XBC)), ("new_ssm_prompt", (1, 1, H, HD, NS)),
         ("new_conf_conv_sample", (1, NB, HIST, D)), ("new_ssm_conv_sample", (1, NB, SH, XBC)),
         ("new_ssm_sample", (1, NB, H, HD, NS))]


def kernel(**inputs):
    import numpy as _np
    import concourse.bacc as _bacc
    from concourse.bass_utils import run_bass_kernel_spmd as _run

    nc = _bacc.Bacc("TRN2", target_bir_lowering=False, num_devices=1)
    arrays, ins, outs = {}, {}, {}
    for name in _INS:
        a = _np.ascontiguousarray(inputs[name])
        arrays[f"in_{name}"] = a
        ins[name] = nc.dram_tensor(f"in_{name}", a.shape, mybir.dt.from_np(a.dtype), kind="ExternalInput").ap()
    for name, shape in _OUTS:
        outs[name] = nc.dram_tensor(f"out_{name}", shape, F32, kind="ExternalOutput").ap()
    build(nc, ins, outs)
    r = _run(nc, [arrays], core_ids=[0])
    return tuple(r.results[0][f"out_{name}"] for name, _ in _OUTS)
```
